# Optimizing a Trainium2 kernel written in Bass

```python
import jax, jax.numpy as jnp
from jax import lax
import numpy as np

D_MODEL = 2048
BATCH = 1
SEQ = 512
DEPTH = 1
DEC_BATCH = 1
DEC_SEQ = 32
PAST_LEN = 256

CHUNK = 64
N_META = 16
MIX_WIDTH = D_MODEL
HEAD_DIM = 128
ATTN_WIDTH = MIX_WIDTH // 2
CONV_WIDTH = MIX_WIDTH - ATTN_WIDTH
N_HEADS = ATTN_WIDTH // HEAD_DIM
CONV_GROUP = 128
CONV_K = 3
D_FF = ((8 * D_MODEL // 3 + 255) // 256) * 256
IN_WIDTH = 3 * ATTN_WIDTH + 3 * CONV_WIDTH
SPLITS = [ATTN_WIDTH, 2 * ATTN_WIDTH, 3 * ATTN_WIDTH, 3 * ATTN_WIDTH + CONV_WIDTH, 3 * ATTN_WIDTH + 2 * CONV_WIDTH]
Q_BLOCK = 128
EPS = 1e-6
SB_SCALE = HEAD_DIM ** -0.5

kernel_name = "hymba_stickbreak_shortconv_stream_step"

def rms_norm(x, g):
    xf = x.astype(jnp.float32)
    y = xf * lax.rsqrt(jnp.mean(xf * xf, axis=-1, keepdims=True) + EPS)
    return (y * g.astype(jnp.float32)).astype(x.dtype)

def group_rms_norm(x, g, group):
    shp = x.shape
    n_grp = shp[-1] // group
    y = rms_norm(x.reshape(shp[:-1] + (n_grp, group)), g.reshape(n_grp, group))
    return y.reshape(shp)

def sb_attend(q, k, v, q_pos, k_pos):
    z = jnp.einsum('bqhd,bkhd->bhqk', q, k).astype(jnp.float32) * SB_SCALE
    visible = (k_pos[None, :] < q_pos[:, None])[None, None]
    log_1m_beta = jnp.where(visible, jax.nn.log_sigmoid(-z), 0.0)
    after = lax.cumsum(log_1m_beta, axis=3, reverse=True) - log_1m_beta
    w = jnp.where(visible, jnp.exp(jax.nn.log_sigmoid(z) + after), 0.0)
    return jnp.einsum('bhqk,bkhd->bqhd', w.astype(v.dtype), v)

def sb_attention_prompt(q, k, v):
    b, n, h, dh = q.shape
    n_blk = -(-n // Q_BLOCK)
    pad = n_blk * Q_BLOCK - n
    padw = ((0, 0), (0, pad), (0, 0), (0, 0))
    qp, kp, vp = jnp.pad(q, padw), jnp.pad(k, padw), jnp.pad(v, padw)
    pos = jnp.arange(n_blk * Q_BLOCK)
    q_blocks = qp.reshape(b, n_blk, Q_BLOCK, h, dh).transpose(1, 0, 2, 3, 4)
    pos_blocks = pos.reshape(n_blk, Q_BLOCK)
    out = lax.map(lambda a: sb_attend(a[0], kp, vp, a[1], pos), (q_blocks, pos_blocks))
    return out.transpose(1, 0, 2, 3, 4).reshape(b, n_blk * Q_BLOCK, h, dh)[:, :n]

def sb_attention_cached(q, k, v, k_cache, v_cache):
    p, t = k_cache.shape[1], q.shape[1]
    keys = jnp.concatenate([k_cache.astype(k.dtype), k], axis=1)
    vals = jnp.concatenate([v_cache.astype(v.dtype), v], axis=1)
    return sb_attend(q, keys, vals, p + jnp.arange(t), jnp.arange(p + t))

def short_conv(u, state, w):
    t = u.shape[1]
    ext = jnp.concatenate([state.astype(u.dtype), u], axis=1)
    y = sum(ext[:, i:i + t] * w[i].astype(u.dtype) for i in range(CONV_K))
    return y, ext[:, -(CONV_K - 1):]

def layer(h, attend, conv_state, w_in, w_out, conv_w, g_pre_mix, g_post_mix, g_attn_out,
          g_conv_out, g_pre_ffn, g_post_ffn, w_gate, w_up, w_down):
    b, t, _ = h.shape
    xn = rms_norm(h, g_pre_mix)
    proj = jnp.einsum('btd,de->bte', xn, w_in)
    q, k, v, gate_b, gate_c, conv_in = jnp.split(proj, SPLITS, axis=-1)
    q = q.reshape(b, t, N_HEADS, HEAD_DIM)
    k = k.reshape(b, t, N_HEADS, HEAD_DIM)
    v = v.reshape(b, t, N_HEADS, HEAD_DIM)
    attn = attend(q, k, v).reshape(b, t, ATTN_WIDTH)
    conv_y, conv_last = short_conv(gate_c * conv_in, conv_state, conv_w)
    mix = jnp.concatenate([group_rms_norm(attn, g_attn_out, HEAD_DIM),
                           group_rms_norm(gate_b * conv_y, g_conv_out, CONV_GROUP)], axis=-1)
    h = h + rms_norm(jnp.einsum('bte,ed->btd', mix, w_out), g_post_mix)
    xf = rms_norm(h, g_pre_ffn)
    ff = jax.nn.silu(jnp.einsum('btd,df->btf', xf, w_gate)) * jnp.einsum('btd,df->btf', xf, w_up)
    h = h + rms_norm(jnp.einsum('btf,fd->btd', ff, w_down), g_post_ffn)
    return h, k, v, conv_last

def setup_inputs(seed: int = 0) -> dict:
    key = jax.random.key(seed)
    ks = jax.random.split(key, 20)
    f32 = jnp.float32

    def nrm(k, shape, scale):
        return jax.random.normal(k, shape, f32) * scale

    def gain(k, shape):
        return 1.0 + 0.05 * jax.random.normal(k, shape, f32)

    return {
        "x_prompt": nrm(ks[0], (BATCH, SEQ, D_MODEL), 1.0),
        "x_sample": nrm(ks[1], (DEC_BATCH, DEC_SEQ, D_MODEL), 1.0),
        "cache_k": nrm(ks[2], (DEPTH, DEC_BATCH, PAST_LEN, N_HEADS, HEAD_DIM), 1.0),
        "cache_v": nrm(ks[3], (DEPTH, DEC_BATCH, PAST_LEN, N_HEADS, HEAD_DIM), 1.0),
        "state_conv": nrm(ks[4], (DEPTH, DEC_BATCH, CONV_K - 1, CONV_WIDTH), 1.0),
        "meta": nrm(ks[5], (N_META, D_MODEL), 1.0),
        "w_in": nrm(ks[6], (DEPTH, D_MODEL, IN_WIDTH), D_MODEL ** -0.5),
        "w_out": nrm(ks[7], (DEPTH, MIX_WIDTH, D_MODEL), MIX_WIDTH ** -0.5),
        "conv_w": nrm(ks[8], (DEPTH, CONV_K, CONV_WIDTH), CONV_K ** -0.5),
        "g_pre_mix": gain(ks[9], (DEPTH, D_MODEL)),
        "g_post_mix": gain(ks[10], (DEPTH, D_MODEL)),
        "g_attn_out": gain(ks[11], (DEPTH, ATTN_WIDTH)),
        "g_conv_out": gain(ks[12], (DEPTH, CONV_WIDTH)),
        "g_pre_ffn": gain(ks[13], (DEPTH, D_MODEL)),
        "g_post_ffn": gain(ks[14], (DEPTH, D_MODEL)),
        "w_gate": nrm(ks[15], (DEPTH, D_MODEL, D_FF), D_MODEL ** -0.5),
        "w_up": nrm(ks[16], (DEPTH, D_MODEL, D_FF), D_MODEL ** -0.5),
        "w_down": nrm(ks[17], (DEPTH, D_FF, D_MODEL), D_FF ** -0.5),
    }

def reference(x_prompt, x_sample, cache_k, cache_v, state_conv, meta, w_in, w_out, conv_w,
              g_pre_mix, g_post_mix, g_attn_out, g_conv_out, g_pre_ffn, g_post_ffn,
              w_gate, w_up, w_down):
    b = x_prompt.shape[0]
    hp = jnp.concatenate([jnp.broadcast_to(meta.astype(x_prompt.dtype)[None], (b, N_META, D_MODEL)),
                          x_prompt], axis=1)
    hs = x_sample
    zero_conv = jnp.zeros((b, CONV_K - 1, CONV_WIDTH), hp.dtype)
    kp_l, vp_l, cp_l, ks_l, vs_l, cs_l = [], [], [], [], [], []
    for l in range(DEPTH):
        params = (w_in[l], w_out[l], conv_w[l], g_pre_mix[l], g_post_mix[l], g_attn_out[l],
                  g_conv_out[l], g_pre_ffn[l], g_post_ffn[l], w_gate[l], w_up[l], w_down[l])
        hp, kp, vp, cp = layer(hp, sb_attention_prompt, zero_conv, *params)
        kc, vc = cache_k[l], cache_v[l]
        hs, ks_, vs_, cs_ = layer(hs, lambda q, k, v: sb_attention_cached(q, k, v, kc, vc),
                                  state_conv[l], *params)
        kp_l.append(kp); vp_l.append(vp); cp_l.append(cp)
        ks_l.append(ks_); vs_l.append(vs_); cs_l.append(cs_)
    y_prompt = hp[:, N_META:]
    y_sample = hs
    new_k_prompt = jnp.stack(kp_l)
    new_v_prompt = jnp.stack(vp_l)
    new_conv_prompt = jnp.stack(cp_l)
    new_k_sample = jnp.stack(ks_l)
    new_v_sample = jnp.stack(vs_l)
    new_conv_sample = jnp.stack(cs_l)
    return (y_prompt, y_sample, new_k_prompt, new_v_prompt, new_conv_prompt,
            new_k_sample, new_v_sample, new_conv_sample)


_drawn_inputs = setup_inputs


def setup_inputs(seed=0):
    import zlib

    import numpy as np

    out = dict(_drawn_inputs(seed))
    spreads = {}
    factors = {}
    for name, (base, spread) in spreads.items():
        noise = np.random.default_rng([zlib.crc32(name.encode()), seed]).standard_normal(out[name].shape)
        drawn = base * np.exp(spread * noise) if base else spread * noise
        out[name] = __import__('jax').numpy.asarray(drawn.astype(out[name].dtype))
    for name, factor in factors.items():
        out[name] = (out[name] * factor).astype(out[name].dtype)
    return out
```

```python
from contextlib import ExitStack

import concourse.bass as bass
from concourse import mybir

F32 = mybir.dt.float32
F32R = mybir.dt.float32r
ALU = mybir.AluOpType
ACT = mybir.ActivationFunctionType

P = 128
EPS = 1e-6


def build_layer(nc, x_prompt, x_sample, cache_k, cache_v, state_conv, meta, w_in, w_out, conv_w,
                g_pre_mix, g_post_mix, g_attn_out, g_conv_out, g_pre_ffn, g_post_ffn,
                w_gate, w_up, w_down,
                y_prompt, y_sample, new_k_prompt, new_v_prompt, new_conv_prompt,
                new_k_sample, new_v_sample, new_conv_sample, h_scratch):
    D = x_prompt.shape[2]
    SEQ = x_prompt.shape[1]
    NMETA = meta.shape[0]
    TP = NMETA + SEQ
    TS = x_sample.shape[1]
    T = TP + TS
    HALF = T // 2
    KC = D // P
    HEADS = cache_k.shape[3]
    GROUPS = conv_w.shape[2] // P
    PAST = cache_k.shape[2]
    DFF = w_gate.shape[2]
    TAIL = TP % P
    MAIN = TP - TAIL
    QB = MAIN // P
    SCALE = float(P) ** -0.5
    assert (T % 2, QB, TAIL, TS, PAST, HEADS, GROUPS) == (0, 4, 16, 32, 2 * P, 8, 8)

    TK = 8
    LEAD = 3
    SLOTS = 4
    PAIR_T = 12
    IN_T = PAIR_T * (HEADS + GROUPS) // 2
    OUT_T = 2 * KC
    FB = 4
    NFB = DFF // P // FB
    FF_T = FB * 4 + KC // 2
    FF_CH = 2 * FB + KC
    CH_OUT = IN_T // 2
    CH_FF = CH_OUT + KC
    T_OUT = IN_T
    T_FF = IN_T + OUT_T

    B1, B3 = 512, 512 + 384
    B2 = 1024
    BT = B2 + 256
    BC = BT + QB * TAIL
    BTT = BC + 2 * TS
    BNN = BTT + TAIL
    ZW = BNN + TS
    key_block_at = [0, B1, B2, B3]

    C_STATE, C_CONVW = 0, 16
    C_PREMIX, C_POSTMIX = 40, 56
    C_ATTN, C_CONV = 72, 80
    C_PREFFN, C_POSTFFN = 88, 104
    NCOL = 120

    with ExitStack() as ctx:
        def sb(name, shape, dt=F32):
            return ctx.enter_context(nc.sbuf_tensor(name, shape, dt))

        def sem(name):
            return ctx.enter_context(nc.semaphore(name))

        act_hi = sb("act_hi", [P, KC, T], F32R)
        act_lo = sb("act_lo", [P, KC, T], F32R)
        wide = sb("wide", [P, KC * T])
        wide_c = wide[:, :].rearrange("p (c t) -> p c t", c=KC)
        misc = sb("misc", [P, KC * T])
        resid = misc[:, :].rearrange("p (c t) -> p c t", c=KC)
        w_raw = sb("w_raw", [P, 2560])
        w_hi = sb("w_hi", [P, SLOTS, TK * P], F32R)
        w_lo = sb("w_lo", [P, SLOTS, TK * P], F32R)
        rstd = sb("rstd", [P, T])
        buf_g = sb("buf_g", [P, T])
        buf_e = sb("buf_e", [P, T])
        ff_hi = sb("ff_hi", [P, FB, T], F32R)
        ff_lo = sb("ff_lo", [P, FB, T], F32R)
        ident = sb("ident", [P, P])
        neg1 = sb("neg1", [P, P])
        cols = sb("cols", [P, NCOL])
        eps = sb("eps", [P, 1])

        def carve(at, n):
            return misc[:, at:at + n], at + n

        at = 0
        qT, at = carve(at, 564)
        kT, at = carve(at, 564)
        vT, at = carve(at, 564)
        vtok_f, at = carve(at, 2 * 6 * P)
        ktok_f, at = carve(at, 6 * P)
        soft, at = carve(at, ZW)
        relu, at = carve(at, ZW)
        kc_tok_f, at = carve(at, 2 * P)
        kcT, at = carve(at, 2 * P)
        vc_f, at = carve(at, 2 * P)
        uext, at = carve(at, TP + TS + 4)
        ulast_f, at = carve(at, 4 * GROUPS)
        tri, at = carve(at, P)
        assert at <= KC * T
        vtok = vtok_f.rearrange("p (b j d) -> p b j d", b=2, j=6)
        ktok = ktok_f.rearrange("p (j d) -> p j d", j=6)
        kc_tok = kc_tok_f.rearrange("p (j d) -> p j d", j=2)
        vc = vc_f.rearrange("p (j d) -> p j d", j=2)
        ulast = ulast_f.rearrange("p (a g) -> p a g", a=4)
        x_tok = [wide[:, j * D:(j + 1) * D] for j in range(QB)] + [misc[:, 0:D]]
        h_ring = misc[:, D:D + 4 * T].rearrange("p (s t) -> p s t", s=4)
        col_rows = misc[0:NCOL, D + 4 * T:D + 4 * T + P]
        assert D + 4 * T + P <= at - P
        y_tok = w_raw[:, :].rearrange("p (s j f) -> p s j f", s=4, j=5)

        ps = ctx.enter_context(nc.psum_tensor("ps", [P, 8, 512], F32))
        acc = [ps[:, 2 * s:2 * s + 2, 0:HALF] for s in range(2)]
        bank_a, bank_b, bank_c, bank_d = (ps[:, 4 + j, :] for j in range(4))
        score_banks = [bank_a, bank_b, bank_c]

        x_loaded = [sem(f"x_loaded{j}") for j in range(QB + 1)]
        cols_loaded = sem("cols_loaded")
        const_ready = sem("const_ready")
        pool_step = sem("pool_step")
        cols_turned = sem("cols_turned")
        cols_ready = sem("cols_ready")
        x_turned = sem("x_turned")
        h_left = sem("h_left")
        h_right = sem("h_right")
        x_hi_ready = sem("x_hi_ready")
        x_ready = sem("x_ready")
        h_stored = [sem(f"h_stored{j}") for j in range(4)]
        sq_made = sem("sq_made")
        sq_added = sem("sq_added")
        ms_ready = sem("ms_ready")
        ms_log = sem("ms_log")
        rstd_ready = sem("rstd_ready")
        w_loaded = [sem(f"w_loaded{j}") for j in range(2)]
        hi_ready = sem("hi_ready")
        lo_ready = sem("lo_ready")
        first_used = sem("first_used")
        chunk_done = sem("chunk_done")
        chunk_copied = sem("chunk_copied")
        kc_loaded = sem("kc_loaded")
        vc_loaded = sem("vc_loaded")
        kc_turned = sem("kc_turned")
        kc_copied = sem("kc_copied")
        v_turned = sem("v_turned")
        v_copied = sem("v_copied")
        k_turned = sem("k_turned")
        k_copied = sem("k_copied")
        ends_turned = sem("ends_turned")
        ends_copied = sem("ends_copied")
        k_stored = sem("k_stored")
        v_stored = [sem(f"v_stored{j}") for j in range(2)]
        z_ready = sem("z_ready")
        abs_ready = sem("abs_ready")
        exp_ready = sem("exp_ready")
        log_ready = sem("log_ready")
        sp_made = sem("sp_made")
        sp_ready = sem("sp_ready")
        e_ready = sem("e_ready")
        w_made = sem("w_made")
        w_ready = sem("w_ready")
        o_ready = sem("o_ready")
        o_copied = sem("o_copied")
        sq_ready = sem("sq_ready")
        n1_ready = sem("n1_ready")
        n1_log = sem("n1_log")
        n2_ready = sem("n2_ready")
        n2_log = sem("n2_log")
        norm_ready = sem("norm_ready")
        mixed = sem("mixed")
        bank_c_clear = sem("bank_c_clear")
        c_scaled = sem("c_scaled")
        u_ends = sem("u_ends")
        conv_step = sem("conv_step")
        ulast_turned = sem("ulast_turned")
        ulast_copied = sem("ulast_copied")
        conv_stored = sem("conv_stored")
        mix_hi = sem("mix_hi")
        mix_split = [sem("mix_split0"), sem("mix_split1")]
        h_loaded = sem("h_loaded")
        scaled = sem("scaled")
        h2_ready = sem("h2_ready")
        f_hi = sem("f_hi")
        f_split = sem("f_split")
        e_neg = sem("e_neg")
        ff_step = sem("ff_step")
        ff_hi_ready = sem("ff_hi_ready")
        ff_ready = sem("ff_ready")
        y_scaled = sem("y_scaled")
        y_ready = sem("y_ready")
        y_turned = sem("y_turned")
        y_left = sem("y_left")
        y_right = sem("y_right")
        y_stored = [sem(f"y_stored{j}") for j in range(4)]

        def tile_no(phase, k):
            per, r, first = phase
            return r * per + first + k

        def known(x):
            return isinstance(x, int)

        def loads_of(phase, k):
            per, r, first = phase
            return r * (per // 2) + (first + k) // 2 + 1

        def tile_used(phase, k):
            per, r, first = phase
            if per == FF_T:
                if k < 0:
                    return chunk_done, r * FF_CH + CH_FF + 2 * (k + 1)
                if k >= 4 * FB:
                    return chunk_done, r * FF_CH + CH_FF + 2 * FB + 2 * (k - 4 * FB + 1)
                if k % 2:
                    return chunk_done, r * FF_CH + CH_FF + k // 2 + 1
                return first_used, r * 2 * FB + CH_FF + k // 2 + 1
            sem_of = (first_used, chunk_done)[k % 2]
            return sem_of, r * (per // 2) + (first + k) // 2 + 1

        block = ctx.enter_context(nc.Block())

        def raw_slot(k):
            return w_raw[:, (k % 2) * TK * P:(k % 2 + 1) * TK * P]

        def round_weights(phase, k):
            t = tile_no(phase, k)
            nc.scalar.wait_ge(w_loaded[k % 2], 16 * loads_of(phase, k))
            if not known(t) or t >= SLOTS:
                nc.scalar.wait_ge(*tile_used(phase, k - SLOTS))
            nc.scalar.copy(w_hi[:, k % SLOTS, :], raw_slot(k)).then_inc(hi_ready, 1)

        def rest_of_weights(phase, k):
            t = tile_no(phase, k)
            nc.vector.wait_ge(hi_ready, t + 1)
            nc.vector.tensor_tensor(w_lo[:, k % SLOTS, :], raw_slot(k),
                                    w_hi[:, k % SLOTS, :].bitcast(F32),
                                    ALU.subtract).then_inc(lo_ready, 1)

        def multiply(slot, nk, width, col, x_hi, x_lo, x_at, out, ks, first, last):
            hi = w_hi[:, slot, :].rearrange("p (k n) -> p k n", k=nk)
            lo = w_lo[:, slot, :].rearrange("p (k n) -> p k n", k=nk)
            for k in ks:
                for w, x, begins, ends in ((hi, x_hi, first and k == 0, False), (hi, x_lo, False, False),
                                           (lo, x_hi, False, last and k == nk - 1)):
                    for h in range(2):
                        mm = nc.tensor.matmul(out[:, h, :], w[:, k, col:col + width],
                                              x[:, x_at + k, h * HALF:(h + 1) * HALF],
                                              start=begins, stop=ends)
            return mm

        w_in_v = w_in[0].rearrange("(k p) n -> p k n", p=P)
        w_out_v = w_out[0].rearrange("(k p) n -> p k n", p=P)
        w_gate_v = w_gate[0].rearrange("(k p) n -> p k n", p=P)
        w_up_v = w_up[0].rearrange("(k p) n -> p k n", p=P)
        w_down_v = w_down[0].rearrange("(b k p) n -> p b k n", k=FB, p=P)
        AW = HEADS * P
        h_scr = h_scratch

        @block.sync
        def _(sp):
            xp = x_prompt[0]
            sp.dma_start(x_tok[0][0:NMETA, :], meta).then_inc(x_loaded[0], 16)
            sp.dma_start(x_tok[0][NMETA:P, :], xp[0:P - NMETA, :]).then_inc(x_loaded[0], 16)
            sp.dma_start(x_tok[1], xp[P - NMETA:2 * P - NMETA, :]).then_inc(x_loaded[1], 16)
            for rows, at_col in ((state_conv[0, 0], C_STATE), (conv_w[0], C_CONVW),
                                 (g_pre_mix, C_PREMIX), (g_post_mix, C_POSTMIX),
                                 (g_attn_out, C_ATTN), (g_conv_out, C_CONV),
                                 (g_pre_ffn, C_PREFFN), (g_post_ffn, C_POSTFFN)):
                rows = rows.rearrange("a (g p) -> (a g) p", p=P)
                sp.dma_start(col_rows[at_col:at_col + rows.shape[0], :], rows).then_inc(cols_loaded, 16)
            for j in range(2, QB):
                sp.dma_start(x_tok[j], xp[j * P - NMETA:(j + 1) * P - NMETA, :]).then_inc(x_loaded[j], 16)
            sp.dma_start(x_tok[QB][0:TAIL, :], xp[SEQ - TAIL:SEQ, :]).then_inc(x_loaded[QB], 16)
            sp.dma_start(x_tok[QB][TAIL:TAIL + TS, :], x_sample[0]).then_inc(x_loaded[QB], 16)

            def load(phase, k, src):
                t = tile_no(phase, k)
                if not known(t) or t >= 2:
                    sp.wait_ge(lo_ready, t - 1)
                dst = raw_slot(k).rearrange("p (k n) -> p k n", k=src.shape[-2])
                sp.dma_start(dst, src).then_inc(w_loaded[k % 2], 16)

            def load_pair(p, bases):
                phase = (PAIR_T, p, 0)
                q = 2 * (p if bases[0] < 3 * AW else p - HEADS // 2)
                for k in range(PAIR_T):
                    u, c, half = k // 6, k % 6 // 2, k % 2
                    load(phase, k, w_in_v[:, TK * half:TK * (half + 1), :]
                         .rearrange("p k (h n) -> p k h n", n=P)[:, :, bass.ds(q + bases[c] // P + u, 1), :]
                         .rearrange("p k h n -> p k (h n)"))

            HEAD_COLS = (2 * AW, AW, 0)
            CONV_COLS = (3 * AW, 3 * AW + GROUPS * P, 3 * AW + 2 * GROUPS * P)
            phase0 = (PAIR_T, 0, 0)
            for k in range(2):
                load(phase0, k, w_in_v[:, TK * k:TK * (k + 1), 2 * AW:2 * AW + P])
            for c in range(KC):
                sp.wait_ge(h_left, c + 1)
                sp.wait_ge(h_right, c + 1)
                sp.dma_start(h_scr[:, c, :], h_ring[:, c % 4, :]).then_inc(h_stored[c % 4], 16)
            for k in range(2, PAIR_T):
                u, c, half = k // 6, k % 6 // 2, k % 2
                load(phase0, k, w_in_v[:, TK * half:TK * (half + 1),
                                       HEAD_COLS[c] + u * P:HEAD_COLS[c] + (u + 1) * P])
            with sp.Fori(0, HEADS // 2 - 1) as r:
                load_pair(r + 1, HEAD_COLS)
            with sp.Fori(HEADS // 2, (HEADS + GROUPS) // 2) as p:
                load_pair(p, CONV_COLS)

            def load_out(q):
                at_col = q * 2 * P
                for k in range(4):
                    load((4, q, T_OUT), k, w_out_v[:, TK * (k % 2):TK * (k % 2 + 1),
                                                   bass.ds(at_col + k // 2 * P, P)])
            for q in range(2):
                load_out(q)
            sp.wait_ge(mixed, HEADS + GROUPS)
            sp.wait_ge(conv_stored, 32)
            sp.wait_ge(k_stored, 48 * HEADS)
            for j in range(2):
                sp.wait_ge(v_stored[j], 48 * HEADS // 2)
            for j in range(4):
                sp.wait_ge(h_stored[j], 16 * (KC // 4))
            sp.dma_start(resid, h_scr).then_inc(h_loaded, 16)
            with sp.Fori(2, KC // 2) as q:
                load_out(q)

            with sp.Fori(0, NFB) as b:
                phase = (FF_T, b, T_FF)
                for k in range(4 * FB):
                    f, src = k // 4, (w_gate_v, w_up_v)[k % 4 // 2]
                    load(phase, k, src[:, TK * (k % 2):TK * (k % 2 + 1), bass.ds(b * FB * P + f * P, P)])
                for m in range(KC // 2):
                    load(phase, 4 * FB + m, w_down_v[:, bass.ds(b, 1), :, 2 * P * m:2 * P * (m + 1)]
                         .rearrange("p b k n -> p (b k) n"))

            for c in range(KC):
                s, f = c % 4, slice(c * P, (c + 1) * P)
                sp.wait_ge(y_left, c + 1)
                sp.wait_ge(y_right, c + 1)
                sp.dma_start(y_prompt[0][0:P - NMETA, f], y_tok[NMETA:P, s, 0, :]).then_inc(y_stored[s], 16)
                sp.dma_start(y_prompt[0][P - NMETA:QB * P - NMETA, f].rearrange("(j p) n -> p j n", p=P),
                             y_tok[:, s, 1:QB, :]).then_inc(y_stored[s], 16)
                sp.dma_start(y_prompt[0][SEQ - TAIL:SEQ, f], y_tok[0:TAIL, s, QB, :]).then_inc(y_stored[s], 16)
                sp.dma_start(y_sample[0][:, f], y_tok[TAIL:TAIL + TS, s, QB, :]).then_inc(y_stored[s], 16)
            for s in range(4):
                sp.wait_ge(y_stored[s], 64 * (KC // 4))

        @block.tensor
        def _(pe):
            acts = (act_hi, act_lo)
            hidden = (ff_hi, ff_lo)
            halves_of_tile = (list(range(TK // 2)), list(range(TK // 2, TK)))

            def chunk(phase, k, no, points, x_wait=None):
                if not known(no) or no >= 2:
                    pe.wait_ge(chunk_copied, no - 1)
                out = acc[(k // 2) % 2]
                for half in range(2):
                    pe.wait_ge(lo_ready, tile_no(phase, k + half) + 1)
                    for part in range(2):
                        for kk in halves_of_tile[part]:
                            if x_wait is not None:
                                pe.wait_ge(*x_wait(TK * half + kk))
                            mm = multiply((k + half) % SLOTS, TK, P, 0, *acts, TK * half, out, [kk],
                                          half == 0, half == 1)
                        if part == 0:
                            points[2 * half]()
                    mm.then_inc((first_used, chunk_done)[half], 1)
                    points[2 * half + 1]()

            def turn(out, src, n):
                return nc.tensor.transpose(out, src, ident[0:n, 0:n])

            pe.wait_ge(const_ready, 4)
            pe.wait_ge(cols_loaded, 16 * 8)
            turn(bank_d[:, 0:NCOL], col_rows, NCOL).then_inc(cols_turned, 1)
            for c in range(KC):
                s = c % 4
                if c >= 4:
                    pe.wait_ge(h_left, c - 3)
                    pe.wait_ge(h_right, c - 3)
                if c == 3:
                    pe.wait_ge(cols_ready, 1)
                for j in range(QB + 1):
                    if c == 0:
                        pe.wait_ge(x_loaded[j], 32 if j in (0, QB) else 16)
                    n = P if j < QB else TAIL + TS
                    mm = turn(ps[:, 2 * s + j // 3, (j % 3) * P:(j % 3) * P + n],
                              x_tok[j][0:n, c * P:(c + 1) * P], n)
                mm.then_inc(x_turned, 1)
            pe.wait_ge(h_left, KC)
            pe.wait_ge(h_right, KC)

            def row_sums(r):
                pe.wait_ge(sq_added, KC * (r + 1))
                for h, bank in enumerate((bank_a, bank_b)):
                    mm = nc.tensor.matmul(bank[:, 0:HALF], neg1[:, :], buf_g[:, h * HALF:(h + 1) * HALF],
                                          start=True, stop=True)
                mm.then_inc(ms_ready, 1)

            def into(out, w, x, start=False):
                return nc.tensor.matmul(out, w, x, start=start, stop=True, skip_group_check=True)

            def scores(a):
                pe.wait_ge(chunk_copied, 3 * a + 3)
                pe.wait_ge(kc_copied, a + 1)
                if known(a) and a == 0:
                    pe.wait_ge(bank_c_clear, 1)
                else:
                    pe.wait_ge(o_copied, a)
                into(bank_a[:, 0:512], kT[:, 0:P], qT[:, 0:MAIN], start=True)
                into(bank_b[:, 0:384], kT[:, P:2 * P], qT[:, P:MAIN], start=True)
                into(bank_b[:, 384:512], kT[:, 3 * P:4 * P], qT[:, 3 * P:MAIN])
                into(bank_c[:, 0:256], kT[:, 2 * P:3 * P], qT[:, 2 * P:MAIN], start=True)
                for j in range(QB):
                    at_c = BT - B2 + j * TAIL
                    into(bank_c[:, at_c:at_c + TAIL], kT[:, j * P:(j + 1) * P], qT[:, MAIN:TP])
                for j in range(2):
                    at_c = BC - B2 + j * TS
                    into(bank_c[:, at_c:at_c + TS], kcT[:, j * P:(j + 1) * P], qT[:, TP:T])
                into(bank_c[0:TAIL, BTT - B2:BNN - B2], kT[:, MAIN:TP], qT[:, MAIN:TP])
                into(bank_c[0:TS, BNN - B2:ZW - B2], kT[:, TP:T], qT[:, TP:T]).then_inc(z_ready, 1)

            def exponents(a):
                pe.wait_ge(sp_ready, a + 1)
                into(bank_a[:, 0:512], tri, relu[:, 0:512])
                into(bank_b[:, 0:512], tri, relu[:, 512:1024])
                into(bank_c[:, 0:BTT - B2], tri, relu[:, B2:BTT])
                into(bank_c[0:TAIL, BTT - B2:BNN - B2], tri[0:TAIL, 0:TAIL], relu[0:TAIL, BTT:BNN])
                into(bank_c[0:TS, BNN - B2:ZW - B2], tri[0:TS, 0:TS], relu[0:TS, BNN:ZW])

                def spread(at_c, n, blocks, w, x):
                    return into(bank_c[:, at_c:at_c + blocks * n].rearrange("p (b n) -> p b n", b=blocks), w,
                                x.unsqueeze(1).broadcast_to([x.shape[0], blocks, n]))
                for j in range(1, QB):
                    n = MAIN - j * P
                    later = relu[:, key_block_at[j]:key_block_at[j] + n]
                    for i in range(j):
                        end = key_block_at[i] % 512 + MAIN - i * P
                        into(score_banks[key_block_at[i] // 512][:, end - n:end], neg1[:, :], later)
                    spread(BT - B2, TAIL, j, neg1[:, :], relu[:, BT + j * TAIL:BT + (j + 1) * TAIL])
                spread(BT - B2, TAIL, QB, neg1[0:TAIL, :], relu[0:TAIL, BTT:BNN])
                spread(BC - B2, TS, 1, neg1[:, :], relu[:, BC + TS:BC + 2 * TS])
                spread(BC - B2, TS, 2, neg1[0:TS, :], relu[0:TS, BNN:ZW]).then_inc(e_ready, 1)

            def attend(a, par, bank_free):
                pe.wait_ge(w_ready, a + 1)
                pe.wait_ge(ends_copied, a + 1)
                pe.wait_ge(vc_loaded, 16 * (a + 1))
                pe.wait_ge(*bank_free)
                v = vtok[:, par]
                for j in range(QB):
                    n = MAIN - j * P
                    into(bank_d[:, j * P:MAIN], v[:, j, :], soft[:, key_block_at[j]:key_block_at[j] + n],
                         start=j == 0)
                for j in range(QB):
                    into(bank_c[:, 0:TAIL], v[:, j, :], soft[:, BT + j * TAIL:BT + (j + 1) * TAIL],
                         start=j == 0)
                into(bank_c[:, 0:TAIL], v[0:TAIL, QB, :], soft[0:TAIL, BTT:BNN])
                for j in range(2):
                    into(bank_c[:, TAIL:TAIL + TS], vc[:, j, :], soft[:, BC + j * TS:BC + (j + 1) * TS])
                into(bank_c[:, TAIL:TAIL + TS], v[0:TS, QB + 1, :], soft[0:TS, BNN:ZW]).then_inc(o_ready, 1)

            def norm_main(n, *bank_free):
                pe.wait_ge(sq_ready, n + 1)
                pe.wait_ge(*bank_free)
                into(bank_d[:, 0:MAIN], neg1[:, :], buf_e[:, 0:MAIN], start=True).then_inc(n1_ready, 1)

            def norm_ends(n, bank=None):
                if bank is None:
                    pe.wait_ge(n1_log, n + 1)
                    bank = bank_d
                into(bank[:, 256:256 + T - MAIN], neg1[:, :], buf_e[:, MAIN:T], start=True)\
                    .then_inc(n2_ready, 1)

            def turn_cache(i, *bank_free):
                pe.wait_ge(kc_loaded, 16 * (i + 1))
                pe.wait_ge(*bank_free)
                for j in range(2):
                    mm = turn(bank_d[:, j * P:(j + 1) * P], kc_tok[:, j, :], P)
                mm.then_inc(kc_turned, 1)

            def turn_main(src, done, copied, bank_free):
                pe.wait_ge(*copied)
                pe.wait_ge(*bank_free)
                for j in range(QB):
                    mm = turn(bank_d[:, j * P:(j + 1) * P], src[:, j * P:(j + 1) * P], P)
                mm.then_inc(done, 1)

            def turn_ends(i):
                pe.wait_ge(k_copied, i + 1)
                for j, src in enumerate((vT, kT)):
                    turn(bank_d[0:TAIL, j * P:(j + 1) * P], src[:, MAIN:TP], P)
                    mm = turn(bank_d[0:TS, (2 + j) * P:(3 + j) * P], src[:, TP:T], P)
                mm.then_inc(ends_turned, 1)

            def walk(p, u, i, at_point, x_wait=None):
                for c in range(3):
                    points = [at_point.get(4 * c + m, lambda: None) for m in range(1, 5)]
                    chunk((PAIR_T, p, 0), 6 * u + 2 * c, 3 * i + c, points, x_wait if c == 0 else None)

            def head(p, u, i, has_attention, has_norm):
                a, n = i - 1, i - 2

                def after_first_tile():
                    if has_attention:
                        scores(a)
                    if has_norm:
                        norm_main(n, ends_copied, i)

                def after_v():
                    if has_norm:
                        norm_ends(n)
                        pe.wait_ge(n2_log, n + 1)
                    turn_cache(i, *((ends_copied, i) if has_attention else (cols_ready, 1)))

                at_point = {
                    2: after_first_tile,
                    4: after_v,
                    6: lambda: turn_main(vT, v_turned, (chunk_copied, 3 * i + 1), (kc_copied, i + 1)),
                    11: lambda: turn_main(kT, k_turned, (chunk_copied, 3 * i + 2),
                                          (o_copied, i) if has_attention else (v_copied, i + 1)),
                }
                if has_attention:
                    at_point[1] = lambda: turn_ends(a)
                    at_point[7] = lambda: exponents(a)
                    at_point[9] = lambda: attend(a, (u + 1) % 2, (v_copied, i + 1))
                else:
                    at_point[3] = lambda: row_sums(0)
                walk(p, u, i, at_point, None if has_attention else lambda c: (x_ready, c + 1))

            def group(p, u, i, first_pair=False):
                last = HEADS - 1
                if first_pair and u == 0:
                    def after_first_tile():
                        scores(last)
                        norm_main(last - 1, ends_copied, HEADS)
                    at_point = {1: lambda: turn_ends(last), 2: after_first_tile,
                                4: lambda: norm_ends(last - 1), 7: lambda: exponents(last),
                                9: lambda: attend(last, last % 2, (n2_log, last))}
                else:
                    at_point = {6: lambda: norm_main(i - 1, n2_log, i - 1), 8: lambda: norm_ends(i - 1)}
                    if first_pair:
                        at_point[2] = lambda: norm_main(last, o_copied, HEADS)
                        at_point[4] = lambda: norm_ends(last)
                walk(p, u, i, at_point)

            for u in range(2):
                head(0, u, u, u > 0, False)
            with pe.Fori(1, HEADS // 2) as p:
                for u in range(2):
                    head(p, u, 2 * p + u, True, True)
            for u in range(2):
                group(HEADS // 2, u, HEADS + u, first_pair=True)
            with pe.Fori(HEADS // 2 + 1, (HEADS + GROUPS) // 2) as p:
                for u in range(2):
                    group(p, u, 2 * p + u)

            no_points = [lambda: None] * 4

            def last_norm_and_rows():
                norm_main(HEADS + GROUPS - 1, n2_log, HEADS + GROUPS - 1)
                norm_ends(HEADS + GROUPS - 1, bank_c)
                pe.wait_ge(u_ends, GROUPS)
                turn(bank_a[0:4 * GROUPS, 0:P], ulast_f, P).then_inc(ulast_turned, 1)

            def mix_chunk(c):
                return mix_split[c // TK], c % TK + 1

            for c in range(2):
                chunk((4, 0, T_OUT), 2 * c, CH_OUT + c,
                      [lambda: None, last_norm_and_rows] + no_points[2:] if c == 0 else no_points,
                      mix_chunk if c == 0 else None)
            with pe.Fori(1, KC // 2) as q:
                for c in range(2):
                    chunk((4, q, T_OUT), 2 * c, 2 * q + CH_OUT + c, no_points)
            row_sums(1)

            def ffn_block(b, first):
                phase = (FF_T, b, T_FF)
                ch = b * FF_CH + CH_FF
                for j in range(2 * FB):
                    begins = first and j == 0
                    chunk(phase, 2 * j, ch + j,
                          no_points[:3] + [lambda: row_sums(2)] if begins else no_points,
                          (lambda c: (f_split, c + 1)) if begins else None)
                for m in range(KC // 2):
                    k = 4 * FB + m
                    pe.wait_ge(lo_ready, tile_no(phase, k) + 1)
                    for o in range(2):
                        no = ch + 2 * FB + 2 * m + o
                        pe.wait_ge(chunk_copied, no - 1)
                        for kk in range(FB):
                            if m == 0 and o == 0:
                                pe.wait_ge(ff_ready, b * FB + kk + 1)
                            mm = multiply(k % SLOTS, FB, P, o * P, *hidden, 0, acc[o], [kk], True, True)
                        mm.then_inc(chunk_done, 1)

            ffn_block(0, True)
            with pe.Fori(1, NFB) as b:
                ffn_block(b, False)

            row_sums(3)
            for c in range(KC):
                s = c % 4
                pe.wait_ge(y_ready, c + 1)
                if c >= 4:
                    pe.wait_ge(y_left, c - 3)
                    pe.wait_ge(y_right, c - 3)
                for j in range(QB + 1):
                    n = P if j < QB else TAIL + TS
                    mm = turn(ps[0:n, 2 * s + j // 3, (j % 3) * P:(j % 3 + 1) * P],
                              resid[:, c, j * P:j * P + n], P)
                mm.then_inc(y_turned, 1)

        @block.scalar
        def _(act):
            A = nc.scalar.activation
            kp = new_k_prompt[0, 0].rearrange("t h d -> h t d")
            vp = new_v_prompt[0, 0].rearrange("t h d -> h t d")
            ks = new_k_sample[0, 0].rearrange("t h d -> h t d")
            vs = new_v_sample[0, 0].rearrange("t h d -> h t d")
            kc_v = cache_k[0, 0].rearrange("(j p) h d -> p j h d", p=P)
            vc_v = cache_v[0, 0].rearrange("(j p) h d -> p j h d", p=P)

            def load_cache(cache, i, dst, done):
                act.dma_start(dst, cache[:, :, bass.ds(i, 1), :].rearrange("p j h d -> p (j h) d"))\
                   .then_inc(done, 16)

            def store_head(prompt, sample, i, src, done):
                act.dma_start(prompt[bass.ds(i, 1), 0:MAIN, :].rearrange("h (j p) d -> p (h j) d", p=P),
                              src[:, 0:QB, :]).then_inc(done, 16)
                act.dma_start(prompt[bass.ds(i, 1), MAIN:TP, :].rearrange("h p d -> p (h d)"),
                              src[0:TAIL, QB, :]).then_inc(done, 16)
                act.dma_start(sample[bass.ds(i, 1), :, :].rearrange("h p d -> p (h d)"),
                              src[0:TS, QB + 1, :]).then_inc(done, 16)

            def make_rstd(r):
                act.wait_ge(ms_ready, r + 1)
                A(rstd[:, :].rearrange("p (h t) -> p h t", h=2), ps[:, 4:6, 0:HALF], ACT.Ln,
                  scale=-1.0 / D, bias=eps[:, 0:1]).then_inc(ms_log, 1)
                act.wait_ge(ms_log, r + 1)
                A(rstd[:, :], rstd[:, :], ACT.Exp, scale=-0.5).then_inc(rstd_ready, 1)

            def norm_log_main(n):
                act.wait_ge(n1_ready, n + 1)
                A(buf_e[:, 0:MAIN], bank_d[:, 0:MAIN], ACT.Ln, scale=-1.0 / P, bias=eps[:, 0:1])\
                    .then_inc(n1_log, 1)

            def norm_finish(n, bank=bank_d):
                act.wait_ge(n2_ready, n + 1)
                A(buf_e[:, MAIN:T], bank[:, 256:256 + T - MAIN], ACT.Ln, scale=-1.0 / P, bias=eps[:, 0:1])\
                    .then_inc(n2_log, 1)
                act.wait_ge(n2_log, n + 1)
                A(buf_e[:, :], buf_e[:, :], ACT.Exp, scale=-0.5).then_inc(norm_ready, 1)

            parts = ((bank_a, 0, 512), (bank_b, 512, 512), (bank_c, B2, ZW - B2))

            def soft_begin(a):
                act.wait_ge(z_ready, a + 1)
                for bank, at_z, n in parts:
                    A(soft[:, at_z:at_z + n], bank[:, 0:n], ACT.Abs)
                for bank, at_z, n in parts:
                    last = A(relu[:, at_z:at_z + n], bank[:, 0:n], ACT.Relu)
                last.then_inc(abs_ready, 1)

            def soft_finish(a):
                act.wait_ge(abs_ready, a + 1)
                A(soft, soft, ACT.Exp, scale=-1.0).then_inc(exp_ready, 1)
                act.wait_ge(exp_ready, a + 1)
                A(soft, soft, ACT.Ln, bias=1.0).then_inc(log_ready, 1)

            def weights_of(a):
                act.wait_ge(e_ready, a + 1)
                for bank, at_z, n in parts:
                    last = A(soft[:, at_z:at_z + n], bank[:, 0:n], ACT.Exp)
                last.then_inc(w_made, 1)

            def square_mix(src, n, ready):
                act.wait_ge(*ready)
                if not known(n) or n > 0:
                    act.wait_ge(mixed, n)
                A(buf_e[:, :], src, ACT.Square).then_inc(sq_ready, 1)

            def square_row(src, r, c, buf_free=None, before=None):
                if buf_free is not None:
                    act.wait_ge(*buf_free)
                act.wait_ge(sq_added, KC * r + c if before is None else before)
                A(buf_e[:, :], src, ACT.Square).then_inc(sq_made, 1)

            for k in range(2):
                round_weights((PAIR_T, 0, 0), k)
            for c in range(KC):
                s = c % 4
                act.wait_ge(x_turned, c + 1)
                if c >= 4:
                    act.wait_ge(h_stored[s], 16 * (c // 4))
                    act.wait_ge(x_ready, c - 3)
                    act.wait_ge(sq_made, c - 3)
                A(h_ring[:, s, 3 * P:T], ps[:, 2 * s + 1, 0:T - 3 * P], ACT.Copy).then_inc(h_right, 1)
                if c == 0:
                    act.wait_ge(cols_ready, 1)
                act.wait_ge(h_left, c + 1)
                act.wait_ge(h_right, c + 1)
                A(act_hi[:, c, :], h_ring[:, s, :], ACT.Copy, scale=cols[:, C_PREMIX + c:C_PREMIX + c + 1])\
                    .then_inc(x_hi_ready, 1)
            round_weights((PAIR_T, 0, 0), 2)

            def head(p, u, i, has_attention, has_norm):
                a, n = i - 1, i - 2
                for s in range(6):
                    round_weights((PAIR_T, p, 0), 6 * u + s + LEAD)
                    if s == 0:
                        if has_attention:
                            act.wait_ge(kc_turned, i)
                        load_cache(kc_v, i, kc_tok, kc_loaded)
                        if has_norm:
                            norm_log_main(n)
                        if has_attention:
                            soft_begin(a)
                    if s == 1:
                        if not has_attention:
                            make_rstd(0)
                        if has_norm:
                            norm_finish(n)
                        if has_attention:
                            soft_finish(a)
                            act.wait_ge(ends_copied, a + 1)
                            store_head(kp, ks, a, ktok, k_stored)
                            store_head(vp, vs, a, vtok[:, (u + 1) % 2], v_stored[(u + 1) % 2])
                    if s == 3 and has_attention:
                        weights_of(a)
                    if s == 4:
                        if has_attention:
                            square_mix(buf_g[:, :], a, (o_copied, a + 1))
                            act.wait_ge(o_ready, i)
                        load_cache(vc_v, i, vc, vc_loaded)

            def group(p, u, i, first_pair=False):
                last = HEADS - 1
                for s in range(6):
                    round_weights((PAIR_T, p, 0), 6 * u + s + LEAD)
                    if first_pair and u == 0:
                        if s == 0:
                            norm_log_main(last - 1)
                            soft_begin(last)
                        if s == 1:
                            norm_finish(last - 1)
                            soft_finish(last)
                            act.wait_ge(ends_copied, HEADS)
                            store_head(kp, ks, last, ktok, k_stored)
                            store_head(vp, vs, last, vtok[:, last % 2], v_stored[last % 2])
                        if s == 3:
                            weights_of(last)
                        if s == 4:
                            square_mix(buf_g[:, :], last, (o_copied, HEADS))
                        continue
                    if first_pair and s == 0:
                        norm_log_main(last)
                    if s == 1:
                        if first_pair:
                            norm_finish(last)
                        square_mix(vT[:, 0:T], i - 1, (conv_step, 4 * (i - HEADS)))
                    if s == 2:
                        norm_log_main(i - 1)
                    if s == 3:
                        norm_finish(i - 1)

            for u in range(2):
                head(0, u, u, u > 0, False)
            with act.Fori(1, HEADS // 2) as p:
                for u in range(2):
                    head(p, u, 2 * p + u, True, True)
            for u in range(2):
                group(HEADS // 2, u, HEADS + u, first_pair=True)
            with act.Fori(HEADS // 2 + 1, (HEADS + GROUPS) // 2) as p:
                for u in range(2):
                    group(p, u, 2 * p + u)

            def mix_high(c):
                act.wait_ge(mixed, c + 1)
                nc.scalar.copy(act_hi[:, c, :], wide_c[:, c, :]).then_inc(mix_hi, 1)

            end = HEADS + GROUPS
            act.wait_ge(chunk_done, 3 * end)
            for c in range(6):
                mix_high(c)
            round_weights((4, 0, T_OUT), LEAD)
            square_mix(vT[:, 0:T], end - 1, (conv_step, 4 * GROUPS))
            for c in range(6, 12):
                mix_high(c)
            norm_log_main(end - 1)
            norm_finish(end - 1, bank_c)
            round_weights((4, 0, T_OUT), LEAD + 1)
            for c in range(12, KC):
                mix_high(c)
            act.wait_ge(ulast_copied, 1)
            rows = relu[0:4 * GROUPS, 0:P]
            act.dma_start(new_conv_prompt[0, 0].rearrange("a (g p) -> (a g) p", p=P), rows[0:2 * GROUPS, :])\
               .then_inc(conv_stored, 16)
            act.dma_start(new_conv_sample[0, 0].rearrange("a (g p) -> (a g) p", p=P),
                          rows[2 * GROUPS:4 * GROUPS, :]).then_inc(conv_stored, 16)

            def out_round(q, k_from):
                for k in range(4):
                    if k >= k_from:
                        round_weights((4, q, T_OUT), k + LEAD)
                    if k % 2:
                        c = 2 * q + k // 2
                        act.wait_ge(chunk_copied, c + CH_OUT + 1)
                        square_row(wide_c[:, bass.ds(c, 1), :].rearrange("p c t -> p (c t)"), 1, c,
                                   (mixed, HEADS + GROUPS))
            out_round(0, 2)
            with act.Fori(1, KC // 2) as q:
                out_round(q, 0)

            make_rstd(1)
            with act.Fori(2 * KC, 3 * KC) as squares:
                c = squares - 2 * KC
                h = resid[:, bass.ds(c, 1), :]
                act.wait_ge(chunk_done, CH_FF)
                act.wait_ge(h2_ready, c + 1)
                A(act_hi[:, bass.ds(c, 1), :], h, ACT.Copy, scale=cols[:, bass.ds(c + C_PREFFN, 1)])\
                    .then_inc(f_hi, 1)
                square_row(h.rearrange("p c t -> p (c t)"), 2, c, (ms_ready, 2), squares)
            make_rstd(2)

            def ffn_block(b, last):
                phase = (FF_T, b, T_FF)
                ch = b * FF_CH + CH_FF
                for k in range(FF_T):
                    if not last or k + LEAD < FF_T:
                        round_weights(phase, k + LEAD)
                    f = k // 4
                    if f < FB and k % 4 == 1:
                        act.wait_ge(chunk_copied, ch + 2 * f + 1)
                        A(buf_e[:, :], buf_g[:, :], ACT.Exp, scale=-1.0).then_inc(e_neg, 1)
                    if f < FB and k % 4 == 3:
                        act.wait_ge(chunk_copied, ch + 2 * f + 2)
                        nc.scalar.copy(ff_hi[:, f, :], buf_g[:, :]).then_inc(ff_hi_ready, 1)
                    if last and f >= FB:
                        for c in (2 * (k - 4 * FB), 2 * (k - 4 * FB) + 1):
                            act.wait_ge(chunk_copied, ch + 2 * FB + c + 1)
                            square_row(wide_c[:, c, :], 3, c)

            with act.Fori(0, NFB - 1) as b:
                ffn_block(b, False)
            ffn_block(NFB - 1, True)

            make_rstd(3)
            for c in range(KC):
                s = c % 4
                act.wait_ge(y_turned, c + 1)
                if c >= 4:
                    act.wait_ge(y_stored[s], 64 * (c // 4))
                A(y_tok[:, s, 3, :], ps[:, 2 * s + 1, 0:P], ACT.Copy)
                A(y_tok[0:TAIL + TS, s, QB, :], ps[0:TAIL + TS, 2 * s + 1, P:2 * P], ACT.Copy)\
                    .then_inc(y_right, 1)

        @block.vector
        def _(dve):
            V = nc.vector

            def column(at_col):
                return cols[:, bass.ds(at_col, 1)] if not known(at_col) else cols[:, at_col:at_col + 1]

            def in_halves(x):
                return x.rearrange("p (h t) -> p h t", h=2)

            def copy_chunk(no, par, out, scale=None):
                dve.wait_ge(chunk_done, no + 1)
                if scale is None:
                    ins = V.tensor_tensor(in_halves(out[:, 0:T]), acc[par], in_halves(rstd[:, :]), ALU.mult)
                else:
                    ins = V.scalar_tensor_tensor(out=in_halves(out[:, 0:T]), in0=acc[par], scalar=scale,
                                                 in1=in_halves(rstd[:, :]), op0=ALU.mult, op1=ALU.mult)
                ins.then_inc(chunk_copied, 1)

            def mix(n, src, at_col):
                dve.wait_ge(norm_ready, n + 1)
                out = wide_c[:, bass.ds(n, 1), :].rearrange("p c t -> p (c t)")
                V.scalar_tensor_tensor(out=out, in0=src, scalar=column(at_col), in1=buf_e[:, :],
                                       op0=ALU.mult, op1=ALU.mult).then_inc(mixed, 1)

            def ends(a, par):
                dve.wait_ge(ends_turned, a + 1)
                V.tensor_copy(vtok[0:TAIL, par, QB, :], bank_d[0:TAIL, 0:P])
                V.tensor_copy(ktok[0:TAIL, QB, :], bank_d[0:TAIL, P:2 * P])
                V.tensor_copy(vtok[0:TS, par, QB + 1, :], bank_d[0:TS, 2 * P:3 * P])
                V.tensor_copy(ktok[0:TS, QB + 1, :], bank_d[0:TS, 3 * P:4 * P]).then_inc(ends_copied, 1)

            def softplus(a):
                dve.wait_ge(log_ready, a + 1)
                V.tensor_tensor(relu, relu, soft, ALU.add).then_inc(sp_made, 1)

            def outputs(a):
                dve.wait_ge(o_ready, a + 1)
                V.tensor_copy(buf_g[:, 0:MAIN], bank_d[:, 0:MAIN])
                V.tensor_copy(buf_g[:, MAIN:T], bank_c[:, 0:T - MAIN]).then_inc(o_copied, 1)

            def conv(g):
                dve.wait_ge(u_ends, g + 1)
                taps = [column(g + C_CONVW + GROUPS * j) for j in range(3)]
                for j in range(3):
                    if j:
                        dve.wait_ge(conv_step, 4 * g + j)
                    for to, n, at_u in ((0, TP, 0), (TP, TS, TP + 2)):
                        x = uext[:, at_u + j:at_u + j + n]
                        if j == 0:
                            last = V.tensor_scalar(vT[:, to:to + n], x, taps[0], None, ALU.mult)
                        else:
                            last = V.scalar_tensor_tensor(out=vT[:, to:to + n], in0=x, scalar=taps[j],
                                                          in1=vT[:, to:to + n], op0=ALU.mult, op1=ALU.add)
                    last.then_inc(conv_step, 1)
                dve.wait_ge(conv_step, 4 * g + 3)
                V.tensor_tensor(vT[:, 0:T], vT[:, 0:T], qT[:, 0:T], ALU.mult).then_inc(conv_step, 1)

            def conv_input(no, par, g):
                dve.wait_ge(chunk_done, no + 1)
                dve.wait_ge(c_scaled, g + 1)
                V.tensor_tensor(uext[:, 2:2 + HALF], acc[par][:, 0, :], kT[:, 0:HALF], ALU.mult)
                V.tensor_tensor(uext[:, 2 + HALF:2 + TP], acc[par][:, 1, 0:TP - HALF], kT[:, HALF:TP], ALU.mult)
                V.tensor_tensor(uext[:, 4 + TP:4 + T], acc[par][:, 1, TP - HALF:HALF], kT[:, TP:T],
                                ALU.mult).then_inc(chunk_copied, 1)
                state = cols[:, C_STATE:C_STATE + 2 * GROUPS].rearrange("p (a g) -> p a g", a=2)
                V.tensor_copy(uext[:, 2 + TP:4 + TP].unsqueeze(2), state[:, :, bass.ds(g, 1)])
                dve.wait_ge(chunk_copied, no + 1)
                V.tensor_copy(ulast[:, 0:2, bass.ds(g, 1)], uext[:, TP:2 + TP].unsqueeze(2))
                V.tensor_copy(ulast[:, 2:4, bass.ds(g, 1)], uext[:, 2 + T:4 + T].unsqueeze(2))\
                    .then_inc(u_ends, 1)

            V.memset(eps[:, :], EPS).then_inc(const_ready, 1)
            for k in range(2):
                rest_of_weights((PAIR_T, 0, 0), k)
            dve.wait_ge(cols_turned, 1)
            V.tensor_copy(cols[:, :], bank_d[:, 0:NCOL]).then_inc(cols_ready, 1)
            dve.wait_ge(cols_ready, 1)
            for c in range(KC):
                s = c % 4
                dve.wait_ge(x_turned, c + 1)
                if c >= 4:
                    dve.wait_ge(h_stored[s], 16 * (c // 4))
                    dve.wait_ge(sq_made, c - 3)
                V.tensor_copy(h_ring[:, s, 0:3 * P], ps[:, 2 * s, 0:3 * P]).then_inc(h_left, 1)
                dve.wait_ge(x_hi_ready, c + 1)
                V.scalar_tensor_tensor(out=act_lo[:, c, :], in0=h_ring[:, s, :], scalar=column(C_PREMIX + c),
                                       in1=act_hi[:, c, :].bitcast(F32), op0=ALU.mult,
                                       op1=ALU.subtract).then_inc(x_ready, 1)
            dve.wait_ge(h_right, KC)
            dve.wait_ge(h_left, KC)
            V.memset(bank_c[:, BTT - B2:ZW - B2], 0.0).then_inc(bank_c_clear, 1)
            rest_of_weights((PAIR_T, 0, 0), 2)
            for j in range(4):
                dve.wait_ge(h_stored[j], 16 * (KC // 4))
            V.memset(uext[:, 0:2], 0.0)

            def head(p, u, i, has_attention, has_norm):
                a, n = i - 1, i - 2
                no = 3 * i
                for s in range(6):
                    rest_of_weights((PAIR_T, p, 0), 6 * u + s + LEAD)
                    if s == 0 and has_attention:
                        ends(a, (u + 1) % 2)
                    if s == 1:
                        if not has_attention:
                            dve.wait_ge(rstd_ready, 1)
                        copy_chunk(no, (3 * u) % 2, vT)
                        dve.wait_ge(kc_turned, i + 1)
                        V.tensor_copy(kcT, bank_d[:, 0:2 * P]).then_inc(kc_copied, 1)
                        if has_norm:
                            mix(n, buf_g[:, :], n + C_ATTN)
                        if has_attention:
                            softplus(a)
                    if s == 2:
                        dve.wait_ge(v_turned, i + 1)
                        if has_norm:
                            dve.wait_ge(v_stored[u], 48 * p)
                        V.tensor_copy(vtok[:, u, 0:QB, :], bank_d.rearrange("p (j d) -> p j d", d=P))\
                            .then_inc(v_copied, 1)
                    if s == 3:
                        copy_chunk(no + 1, (3 * u + 1) % 2, kT)
                    if s == 4 and has_attention:
                        outputs(a)
                    if s == 5:
                        copy_chunk(no + 2, (3 * u + 2) % 2, qT, SCALE)
                        dve.wait_ge(k_turned, i + 1)
                        if has_attention:
                            dve.wait_ge(k_stored, 48 * i)
                        V.tensor_copy(ktok[:, 0:QB, :], bank_d.rearrange("p (j d) -> p j d", d=P))\
                            .then_inc(k_copied, 1)

            def group(p, u, i, first_pair=False):
                last, g, no = HEADS - 1, i - HEADS, 3 * i
                begins = first_pair and u == 0
                for s in range(6):
                    rest_of_weights((PAIR_T, p, 0), 6 * u + s + LEAD)
                    if s == 0:
                        if begins:
                            ends(last, last % 2)
                        else:
                            conv(g - 1)
                    if s == 1:
                        if not begins:
                            dve.wait_ge(conv_step, 4 * g)
                        copy_chunk(no, (3 * u) % 2, qT)
                        if begins:
                            mix(last - 1, buf_g[:, :], C_ATTN + last - 1)
                            softplus(last)
                        elif first_pair:
                            mix(last, buf_g[:, :], C_ATTN + last)
                    if s == 3:
                        copy_chunk(no + 1, (3 * u + 1) % 2, kT)
                        dve.wait_ge(chunk_copied, no + 2)
                        V.tensor_tensor(kT[:, 0:T], kT[:, 0:T], rstd[:, :], ALU.mult).then_inc(c_scaled, 1)
                    if s == 4:
                        if begins:
                            outputs(last)
                        else:
                            mix(i - 1, vT[:, 0:T], g - 1 + C_CONV)
                    if s == 5:
                        conv_input(no + 2, (3 * u + 2) % 2, g)

            for u in range(2):
                head(0, u, u, u > 0, False)
            with dve.Fori(1, HEADS // 2) as p:
                for u in range(2):
                    head(p, u, 2 * p + u, True, True)
            for u in range(2):
                group(HEADS // 2, u, HEADS + u, first_pair=True)
            with dve.Fori(HEADS // 2 + 1, (HEADS + GROUPS) // 2) as p:
                for u in range(2):
                    group(p, u, 2 * p + u)

            def mix_rest(c):
                dve.wait_ge(mix_hi, c + 1)
                V.tensor_tensor(act_lo[:, c, :], wide_c[:, c, :], act_hi[:, c, :].bitcast(F32),
                                ALU.subtract).then_inc(mix_split[1], 1)

            rest_of_weights((4, 0, T_OUT), LEAD)
            conv(GROUPS - 1)
            for c in range(TK, 12):
                mix_rest(c)
            rest_of_weights((4, 0, T_OUT), LEAD + 1)
            mix(HEADS + GROUPS - 1, vT[:, 0:T], C_CONV + GROUPS - 1)
            for c in range(12, KC):
                mix_rest(c)
            dve.wait_ge(ulast_turned, 1)
            V.tensor_copy(relu[0:4 * GROUPS, 0:P], bank_a[0:4 * GROUPS, 0:P]).then_inc(ulast_copied, 1)

            def out_round(q, k_from):
                for k in range(4):
                    if k >= k_from:
                        rest_of_weights((4, q, T_OUT), k + LEAD)
                    if k % 2:
                        c = 2 * q + k // 2
                        dve.wait_ge(chunk_done, c + CH_OUT + 1)
                        out = wide_c[:, bass.ds(c, 1), :].rearrange("p c t -> p (c t)")
                        V.tensor_copy(in_halves(out), acc[k // 2]).then_inc(chunk_copied, 1)
            out_round(0, 2)
            with dve.Fori(1, KC // 2) as q:
                out_round(q, 0)

            def scale_row(c, done):
                x = wide_c[:, bass.ds(c, 1), :].rearrange("p c t -> p (c t)")
                g = column(c + (C_POSTMIX if done is scaled else C_POSTFFN))
                V.scalar_tensor_tensor(out=x, in0=x, scalar=g, in1=rstd[:, :], op0=ALU.mult,
                                       op1=ALU.mult).then_inc(done, 1)

            def split_row(c):
                dve.wait_ge(f_hi, c + 1)
                V.scalar_tensor_tensor(out=act_lo[:, bass.ds(c, 1), :].rearrange("p c t -> p (c t)"),
                                       in0=resid[:, bass.ds(c, 1), :].rearrange("p c t -> p (c t)"),
                                       scalar=column(c + C_PREFFN),
                                       in1=act_hi[:, bass.ds(c, 1), :].rearrange("p c t -> p (c t)").bitcast(F32),
                                       op0=ALU.mult, op1=ALU.subtract).then_inc(f_split, 1)
            dve.wait_ge(rstd_ready, 2)
            for c in range(2):
                scale_row(c, scaled)
            with dve.Fori(0, KC - 2) as c:
                scale_row(c + 2, scaled)
                split_row(c)
            for c in range(KC - 2, KC):
                split_row(c)

            def ffn_block(b, first, last):
                phase = (FF_T, b, T_FF)
                ch = b * FF_CH + CH_FF
                for k in range(FF_T):
                    if not last or k + LEAD < FF_T:
                        rest_of_weights(phase, k + LEAD)
                    f = k // 4
                    if f < FB:
                        if k % 4 == 1:
                            if first and f == 0:
                                dve.wait_ge(rstd_ready, 3)
                            else:
                                dve.wait_ge(ff_ready, b * FB + f)
                            copy_chunk(ch + 2 * f, 0, buf_g)
                        step = b * 4 * FB + 4 * f
                        if k % 4 == 2:
                            dve.wait_ge(e_neg, b * FB + f + 1)
                            V.tensor_scalar(buf_e[:, :], buf_e[:, :], 1.0, None, ALU.add).then_inc(ff_step, 1)
                            dve.wait_ge(ff_step, step + 1)
                            V.reciprocal(buf_e[:, :], buf_e[:, :]).then_inc(ff_step, 1)
                            dve.wait_ge(ff_step, step + 2)
                            V.tensor_tensor(buf_g[:, :], buf_g[:, :], buf_e[:, :], ALU.mult).then_inc(ff_step, 1)
                            dve.wait_ge(ff_step, step + 3)
                            V.tensor_tensor(buf_g[:, :], buf_g[:, :], rstd[:, :], ALU.mult).then_inc(ff_step, 1)
                        if k % 4 == 3:
                            dve.wait_ge(ff_step, step + 4)
                            dve.wait_ge(chunk_done, ch + 2 * f + 2)
                            V.tensor_tensor(in_halves(buf_g[:, :]), acc[1], in_halves(buf_g[:, :]), ALU.mult)\
                                .then_inc(chunk_copied, 1)
                            dve.wait_ge(ff_hi_ready, b * FB + f + 1)
                            V.tensor_tensor(ff_lo[:, f, :], buf_g[:, :], ff_hi[:, f, :].bitcast(F32),
                                            ALU.subtract).then_inc(ff_ready, 1)
                    else:
                        for o in range(2):
                            c = 2 * (k - 4 * FB) + o
                            dve.wait_ge(chunk_done, ch + 2 * FB + c + 1)
                            y = in_halves(wide_c[:, c, :])
                            ins = V.tensor_copy(y, acc[o]) if first else V.tensor_tensor(y, acc[o], y, ALU.add)
                            ins.then_inc(chunk_copied, 1)

            ffn_block(0, True, False)
            with dve.Fori(1, NFB - 1) as b:
                ffn_block(b, False, False)
            ffn_block(NFB - 1, False, True)

            dve.wait_ge(rstd_ready, 4)
            for c in range(3):
                scale_row(c, y_scaled)
            for c in range(KC):
                if c + 3 < KC:
                    scale_row(c + 3, y_scaled)
                s = c % 4
                dve.wait_ge(y_turned, c + 1)
                if c >= 4:
                    dve.wait_ge(y_stored[s], 64 * (c // 4))
                V.tensor_copy(y_tok[:, s, 0:3, :], ps[:, 2 * s, 0:3 * P].rearrange("p (j f) -> p j f", f=P))\
                    .then_inc(y_left, 1)

        def add_square(pool, r, c):
            if c == 0:
                ins = nc.gpsimd.tensor_copy(buf_g[:, :], buf_e[:, :])
            else:
                pool.wait_ge(sq_added, KC * r + c)
                ins = nc.gpsimd.tensor_tensor(buf_g[:, :], buf_g[:, :], buf_e[:, :], ALU.add)
            ins.then_inc(sq_added, 1)

        @block.gpsimd
        def _(pool):
            G = nc.gpsimd
            G.memset(neg1[:, :], -1.0).then_inc(const_ready, 1)
            G.memset(ident[:, :], 0.0).then_inc(pool_step, 1)
            pool.wait_ge(pool_step, 1)
            G.affine_select(out=ident[:, :], in_=ident[:, :], compare_op=ALU.not_equal, fill=1.0, base=0,
                            pattern=[[-1, P]], channel_multiplier=1).then_inc(const_ready, 1)
            pool.wait_ge(const_ready, 3)
            G.affine_select(out=tri, in_=neg1[:, :], compare_op=ALU.is_ge, fill=0.0, base=0,
                            pattern=[[-1, P]], channel_multiplier=1).then_inc(const_ready, 1)

            for c in range(KC):
                s = c % 4
                pool.wait_ge(h_left, c + 1)
                pool.wait_ge(h_right, c + 1)
                if c:
                    pool.wait_ge(sq_added, c)
                G.tensor_tensor(buf_e[:, :], h_ring[:, s, :], h_ring[:, s, :], ALU.mult).then_inc(sq_made, 1)
                pool.wait_ge(sq_made, c + 1)
                add_square(pool, 0, c)

            def mask(buf, made, ready, heads):
                pool.wait_ge(sq_added, KC)
                pool.wait_ge(made, heads)
                for at_z, n in ((0, P), (B1, P), (B3, P), (B2, P), (BTT, TAIL), (BNN, TS)):
                    x = buf[0:n, at_z:at_z + n]
                    last = G.affine_select(out=x, in_=x, compare_op=ALU.is_gt, fill=0.0, base=0,
                                           pattern=[[1, n]], channel_multiplier=-1)
                last.then_inc(ready, 1)

            with pool.Fori(1, HEADS + 1) as heads:
                mask(relu, sp_made, sp_ready, heads)
                mask(soft, w_made, w_ready, heads)

            for c in range(TK):
                pool.wait_ge(mix_hi, c + 1)
                G.tensor_tensor(act_lo[:, c, :], wide_c[:, c, :], act_hi[:, c, :].bitcast(F32),
                                ALU.subtract).then_inc(mix_split[0], 1)

            for c in range(KC):
                pool.wait_ge(sq_made, KC + c + 1)
                add_square(pool, 1, c)

            pool.wait_ge(h_loaded, 16)
            for c in range(KC):
                pool.wait_ge(scaled, c + 1)
                G.tensor_tensor(resid[:, c, :], resid[:, c, :], wide_c[:, c, :], ALU.add).then_inc(h2_ready, 1)
                if c:
                    pool.wait_ge(sq_made, 2 * KC + c)
                    add_square(pool, 2, c - 1)
            pool.wait_ge(sq_made, 3 * KC)
            add_square(pool, 2, KC - 1)

            for c in range(KC):
                pool.wait_ge(sq_made, 3 * KC + c + 1)
                add_square(pool, 3, c)
            for c in range(KC):
                pool.wait_ge(y_scaled, c + 1)
                G.tensor_tensor(resid[:, c, :], resid[:, c, :], wide_c[:, c, :], ALU.add).then_inc(y_ready, 1)


_INS = ["x_prompt", "x_sample", "cache_k", "cache_v", "state_conv", "meta", "w_in", "w_out", "conv_w",
        "g_pre_mix", "g_post_mix", "g_attn_out", "g_conv_out", "g_pre_ffn", "g_post_ffn",
        "w_gate", "w_up", "w_down"]


def kernel(**inputs):
    import numpy as _np
    import concourse.bacc as _bacc
    from concourse import mybir as _mybir
    from concourse.bass_utils import run_bass_kernel_spmd as _run

    arrays = {f"in_{n}_dram": _np.ascontiguousarray(inputs[n]) for n in _INS}
    nc = _bacc.Bacc("TRN2", target_bir_lowering=False, num_devices=1)
    args = [nc.dram_tensor(n, a.shape, _mybir.dt.from_np(a.dtype), kind="ExternalInput").ap()
            for n, a in arrays.items()]
    _, seq, d = inputs["x_prompt"].shape
    _, ts, _ = inputs["x_sample"].shape
    tp = inputs["meta"].shape[0] + seq
    depth, _, _, heads, hd = inputs["cache_k"].shape
    state = inputs["state_conv"].shape
    outs = [(1, seq, d), (1, ts, d), (depth, 1, tp, heads, hd), (depth, 1, tp, heads, hd), state,
            (depth, 1, ts, heads, hd), (depth, 1, ts, heads, hd), state]
    for i, shape in enumerate(outs):
        args.append(nc.dram_tensor(f"out_{i}_dram", shape, _mybir.dt.float32, kind="ExternalOutput").ap())
    args.append(nc.dram_tensor("h_scratch", (128, d // 128, tp + ts), _mybir.dt.float32, kind="Internal").ap())
    build_layer(nc, *args)
    r = _run(nc, [arrays], core_ids=[0])
    return tuple(r.results[0][f"out_{i}_dram"] for i in range(len(outs)))
```

```python
from contextlib import ExitStack

import concourse.bass as bass
from concourse import mybir

F32 = mybir.dt.float32
F32R = mybir.dt.float32r
ALU = mybir.AluOpType
ACT = mybir.ActivationFunctionType

P = 128
EPS = 1e-6


def build_layer(nc, x_prompt, x_sample, cache_k, cache_v, state_conv, meta, w_in, w_out, conv_w,
                g_pre_mix, g_post_mix, g_attn_out, g_conv_out, g_pre_ffn, g_post_ffn,
                w_gate, w_up, w_down,
                y_prompt, y_sample, new_k_prompt, new_v_prompt, new_conv_prompt,
                new_k_sample, new_v_sample, new_conv_sample, h_scratch):
    D = x_prompt.shape[2]
    SEQ = x_prompt.shape[1]
    NMETA = meta.shape[0]
    TP = NMETA + SEQ
    TS = x_sample.shape[1]
    T = TP + TS
    HALF = T // 2
    LATE = slice(NMETA, T)
    LHALF = (T - NMETA) // 2
    KC = D // P
    HEADS = cache_k.shape[3]
    GROUPS = conv_w.shape[2] // P
    PAST = cache_k.shape[2]
    DFF = w_gate.shape[2]
    TAIL = TP % P
    MAIN = TP - TAIL
    QB = MAIN // P
    SCALE = float(P) ** -0.5
    assert ((T - NMETA) % 4, QB, TAIL, TS, PAST, HEADS, GROUPS) == (0, 4, 16, 32, 2 * P, 8, 8)

    TK = 8
    LEAD = 3
    SLOTS = 4
    PAIR_T = 12
    IN_T = PAIR_T * (HEADS + GROUPS) // 2
    OUT_T = 2 * KC
    FB = 4
    NFB = DFF // P // FB
    FF_T = FB * 4 + KC // 2
    FF_CH = 2 * FB + KC
    CH_OUT = IN_T // 2
    CH_FF = CH_OUT + KC
    T_OUT = IN_T
    T_FF = IN_T + OUT_T

    B1, B3 = 512, 512 + 384
    B2 = 1024
    BT = B2 + 256
    BC = BT + QB * TAIL
    BTT = BC + 2 * TS
    BNN = BTT + TAIL
    ZW = BNN + TS
    key_block_at = [0, B1, B2, B3]

    C_STATE, C_CONVW = 0, 16
    C_PREMIX, C_POSTMIX = 40, 56
    C_ATTN, C_CONV = 72, 80
    C_PREFFN, C_POSTFFN = 88, 104
    NCOL = 120

    with ExitStack() as ctx:
        def sb(name, shape, dt=F32):
            return ctx.enter_context(nc.sbuf_tensor(name, shape, dt))

        def sem(name):
            return ctx.enter_context(nc.semaphore(name))

        act_hi = sb("act_hi", [P, KC, T], F32R)
        act_lo = sb("act_lo", [P, KC, T], F32R)
        wide = sb("wide", [P, KC * T])
        wide_c = wide[:, :].rearrange("p (c t) -> p c t", c=KC)
        misc = sb("misc", [P, KC * T])
        resid = misc[:, :].rearrange("p (c t) -> p c t", c=KC)
        w_raw = sb("w_raw", [P, 2560])
        w_hi = sb("w_hi", [P, SLOTS, TK * P], F32R)
        w_lo = sb("w_lo", [P, SLOTS, TK * P], F32R)
        rstd = sb("rstd", [P, T])
        buf_g = sb("buf_g", [P, T])
        buf_e = sb("buf_e", [P, T])
        ff_hi = sb("ff_hi", [P, FB, T], F32R)
        ff_lo = sb("ff_lo", [P, FB, T], F32R)
        ident = sb("ident", [P, P])
        neg1 = sb("neg1", [P, P])
        cols = sb("cols", [P, NCOL])
        eps = sb("eps", [P, 1])
        sq_sums = sb("sq_sums", [P, 2, QB + 1])

        def carve(at, n):
            return misc[:, at:at + n], at + n

        at = 0
        qT, at = carve(at, 564)
        kT, at = carve(at, 564)
        vT, at = carve(at, 564)
        vtok_f, at = carve(at, 2 * 6 * P)
        ktok_f, at = carve(at, 6 * P)
        soft, at = carve(at, ZW)
        relu, at = carve(at, ZW)
        kc_tok_f, at = carve(at, 2 * P)
        kcT, at = carve(at, 2 * P)
        vc_f, at = carve(at, 2 * P)
        uext, at = carve(at, TP + TS + 4)
        ulast_f, at = carve(at, 4 * GROUPS)
        tri, at = carve(at, P)
        assert at <= KC * T
        vtok = vtok_f.rearrange("p (b j d) -> p b j d", b=2, j=6)
        ktok = ktok_f.rearrange("p (j d) -> p j d", j=6)
        kc_tok = kc_tok_f.rearrange("p (j d) -> p j d", j=2)
        vc = vc_f.rearrange("p (j d) -> p j d", j=2)
        ulast = ulast_f.rearrange("p (a g) -> p a g", a=4)
        x_tok = [wide[:, j * D:(j + 1) * D] for j in range(QB)] + [misc[:, 0:D]]
        h_ring = misc[:, D:D + 4 * T].rearrange("p (s t) -> p s t", s=4)
        col_rows = misc[0:NCOL, D + 4 * T:D + 4 * T + P]
        end = D + 4 * T + P
        squares_out = misc[:, end:end + D].rearrange("p (s n) -> p s n", s=2)
        assert end + D <= at - P
        y_tok = w_raw[:, :].rearrange("p (s j f) -> p s j f", s=4, j=5)

        ps = ctx.enter_context(nc.psum_tensor("ps", [P, 8, 512], F32))
        acc = [ps[:, 2 * s:2 * s + 2, 0:HALF] for s in range(2)]
        acc_late = [ps[:, 2 * s:2 * s + 2, 0:LHALF] for s in range(2)]

        def x_bank(c, j):
            n = P if j < QB else TAIL + TS
            return ps[:, 2 + 2 * (c % 3) + j // 3, (j % 3) * P:(j % 3) * P + n]

        bank_a, bank_b, bank_c, bank_d = (ps[:, 4 + j, :] for j in range(4))
        score_banks = [bank_a, bank_b, bank_c]

        x_loaded = [[sem(f"x_loaded{j}_{h}") for h in range(2)] for j in range(QB + 1)]
        cols_loaded = sem("cols_loaded")
        const_ready = sem("const_ready")
        pool_step = sem("pool_step")
        cols_turned = sem("cols_turned")
        cols_ready = sem("cols_ready")
        x_turned = sem("x_turned")
        h_left = sem("h_left")
        h_right = sem("h_right")
        x_hi_ready = sem("x_hi_ready")
        x_ready = sem("x_ready")
        x_squared = sem("x_squared")
        x_summed = sem("x_summed")
        diag_ready = sem("diag_ready")
        h_stored = [sem(f"h_stored{j}") for j in range(4)]
        sq_made = sem("sq_made")
        sq_added = sem("sq_added")
        ms_ready = sem("ms_ready")
        ms_log = sem("ms_log")
        rstd_ready = sem("rstd_ready")
        w_loaded = [sem(f"w_loaded{j}") for j in range(2)]
        hi_ready = sem("hi_ready")
        lo_ready = sem("lo_ready")
        first_used = sem("first_used")
        chunk_done = sem("chunk_done")
        chunk_copied = sem("chunk_copied")
        kc_loaded = sem("kc_loaded")
        vc_loaded = sem("vc_loaded")
        kc_turned = sem("kc_turned")
        kc_copied = sem("kc_copied")
        v_turned = sem("v_turned")
        v_copied = sem("v_copied")
        k_turned = sem("k_turned")
        k_copied = sem("k_copied")
        ends_turned = sem("ends_turned")
        ends_copied = sem("ends_copied")
        k_stored = sem("k_stored")
        v_stored = [sem(f"v_stored{j}") for j in range(2)]
        z_ready = sem("z_ready")
        abs_ready = sem("abs_ready")
        exp_ready = sem("exp_ready")
        log_ready = sem("log_ready")
        sp_made = sem("sp_made")
        sp_ready = sem("sp_ready")
        e_ready = sem("e_ready")
        w_made = sem("w_made")
        w_ready = sem("w_ready")
        o_ready = sem("o_ready")
        o_copied = sem("o_copied")
        sq_ready = sem("sq_ready")
        n1_ready = sem("n1_ready")
        n1_log = sem("n1_log")
        n2_ready = sem("n2_ready")
        n2_log = sem("n2_log")
        norm_ready = sem("norm_ready")
        mixed = sem("mixed")
        bank_c_clear = sem("bank_c_clear")
        c_scaled = sem("c_scaled")
        u_ends = sem("u_ends")
        conv_step = sem("conv_step")
        ulast_turned = sem("ulast_turned")
        ulast_copied = sem("ulast_copied")
        conv_stored = sem("conv_stored")
        mix_hi = sem("mix_hi")
        mix_split = [sem("mix_split0"), sem("mix_split1")]
        h_loaded = sem("h_loaded")
        scaled = sem("scaled")
        h2_ready = sem("h2_ready")
        f_hi = sem("f_hi")
        f_split = sem("f_split")
        e_neg = sem("e_neg")
        ff_step = sem("ff_step")
        ff_hi_ready = sem("ff_hi_ready")
        ff_ready = sem("ff_ready")
        y_scaled = sem("y_scaled")
        y_ready = sem("y_ready")
        y_turned = sem("y_turned")
        y_left = sem("y_left")
        y_right = sem("y_right")
        y_stored = [sem(f"y_stored{j}") for j in range(4)]

        def tile_no(phase, k):
            per, r, first = phase
            return r * per + first + k

        def known(x):
            return isinstance(x, int)

        def loads_of(phase, k):
            per, r, first = phase
            return r * (per // 2) + (first + k) // 2 + 1

        def tile_used(phase, k):
            per, r, first = phase
            if per == FF_T:
                if k < 0:
                    return chunk_done, r * FF_CH + CH_FF + 2 * (k + 1)
                if k >= 4 * FB:
                    return chunk_done, r * FF_CH + CH_FF + 2 * FB + 2 * (k - 4 * FB + 1)
                if k % 2:
                    return chunk_done, r * FF_CH + CH_FF + k // 2 + 1
                return first_used, r * 2 * FB + CH_FF + k // 2 + 1
            sem_of = (first_used, chunk_done)[k % 2]
            return sem_of, r * (per // 2) + (first + k) // 2 + 1

        block = ctx.enter_context(nc.Block())

        def raw_slot(k):
            return w_raw[:, (k % 2) * TK * P:(k % 2 + 1) * TK * P]

        def round_weights(phase, k):
            t = tile_no(phase, k)
            nc.scalar.wait_ge(w_loaded[k % 2], 16 * loads_of(phase, k))
            if not known(t) or t >= SLOTS:
                nc.scalar.wait_ge(*tile_used(phase, k - SLOTS))
            nc.scalar.copy(w_hi[:, k % SLOTS, :], raw_slot(k)).then_inc(hi_ready, 1)

        def rest_of_weights(phase, k):
            t = tile_no(phase, k)
            nc.vector.wait_ge(hi_ready, t + 1)
            nc.vector.tensor_tensor(w_lo[:, k % SLOTS, :], raw_slot(k),
                                    w_hi[:, k % SLOTS, :].bitcast(F32),
                                    ALU.subtract).then_inc(lo_ready, 1)

        def multiply(slot, nk, width, col, x_hi, x_lo, x_at, out, ks, first, last):
            half = out.shape[2]
            token = T - 2 * half
            hi = w_hi[:, slot, :].rearrange("p (k n) -> p k n", k=nk)
            lo = w_lo[:, slot, :].rearrange("p (k n) -> p k n", k=nk)
            for k in ks:
                for w, x, begins, ends in ((hi, x_hi, first and k == 0, False), (hi, x_lo, False, False),
                                           (lo, x_hi, False, last and k == nk - 1)):
                    for h in range(2):
                        mm = nc.tensor.matmul(out[:, h, :], w[:, k, col:col + width],
                                              x[:, x_at + k, token + h * half:token + (h + 1) * half],
                                              start=begins, stop=ends)
            return mm

        w_in_v = w_in[0].rearrange("(k p) n -> p k n", p=P)
        w_out_v = w_out[0].rearrange("(k p) n -> p k n", p=P)
        w_gate_v = w_gate[0].rearrange("(k p) n -> p k n", p=P)
        w_up_v = w_up[0].rearrange("(k p) n -> p k n", p=P)
        w_down_v = w_down[0].rearrange("(b k p) n -> p b k n", k=FB, p=P)
        AW = HEADS * P
        h_scr = h_scratch

        @block.sync
        def _(sp):
            xp = x_prompt[0]

            def load_x(h):
                f = slice(h * D // 2, (h + 1) * D // 2)
                sp.dma_start(x_tok[0][0:NMETA, f], meta[:, f]).then_inc(x_loaded[0][h], 16)
                sp.dma_start(x_tok[0][NMETA:P, f], xp[0:P - NMETA, f]).then_inc(x_loaded[0][h], 16)
                for j in range(1, QB):
                    sp.dma_start(x_tok[j][:, f], xp[j * P - NMETA:(j + 1) * P - NMETA, f])\
                      .then_inc(x_loaded[j][h], 16)
                sp.dma_start(x_tok[QB][0:TAIL, f], xp[SEQ - TAIL:SEQ, f]).then_inc(x_loaded[QB][h], 16)
                sp.dma_start(x_tok[QB][TAIL:TAIL + TS, f], x_sample[0][:, f]).then_inc(x_loaded[QB][h], 16)

            def load(phase, k, src):
                t = tile_no(phase, k)
                if not known(t) or t >= 2:
                    sp.wait_ge(lo_ready, t - 1)
                dst = raw_slot(k).rearrange("p (k n) -> p k n", k=src.shape[-2])
                sp.dma_start(dst, src).then_inc(w_loaded[k % 2], 16)

            def load_pair(p, bases):
                phase = (PAIR_T, p, 0)
                q = 2 * (p if bases[0] < 3 * AW else p - HEADS // 2)
                for k in range(PAIR_T):
                    u, c, half = k // 6, k % 6 // 2, k % 2
                    load(phase, k, w_in_v[:, TK * half:TK * (half + 1), :]
                         .rearrange("p k (h n) -> p k h n", n=P)[:, :, bass.ds(q + bases[c] // P + u, 1), :]
                         .rearrange("p k h n -> p k (h n)"))

            HEAD_COLS = (2 * AW, AW, 0)
            CONV_COLS = (3 * AW, 3 * AW + GROUPS * P, 3 * AW + 2 * GROUPS * P)
            phase0 = (PAIR_T, 0, 0)
            def load_first(k):
                u, c, half = k // 6, k % 6 // 2, k % 2
                load(phase0, k, w_in_v[:, TK * half:TK * (half + 1),
                                       HEAD_COLS[c] + u * P:HEAD_COLS[c] + (u + 1) * P])
            for h in range(2):
                load_x(h)
                load_first(h)
            for c in range(KC):
                if c in (8, 12):
                    load_first(c // 4)
                sp.wait_ge(h_left, c + 1)
                sp.wait_ge(h_right, c + 1)
                sp.dma_start(h_scr[:, c, :], h_ring[:, c % 4, :]).then_inc(h_stored[c % 4], 16)
            for k in range(4, PAIR_T):
                load_first(k)
            with sp.Fori(0, HEADS // 2 - 1) as r:
                load_pair(r + 1, HEAD_COLS)
            with sp.Fori(HEADS // 2, (HEADS + GROUPS) // 2) as p:
                load_pair(p, CONV_COLS)

            def load_out(q):
                at_col = q * 2 * P
                for k in range(4):
                    load((4, q, T_OUT), k, w_out_v[:, TK * (k % 2):TK * (k % 2 + 1),
                                                   bass.ds(at_col + k // 2 * P, P)])
            for q in range(2):
                load_out(q)
            sp.wait_ge(mixed, HEADS + GROUPS)
            sp.wait_ge(conv_stored, 32)
            sp.wait_ge(k_stored, 48 * HEADS)
            for j in range(2):
                sp.wait_ge(v_stored[j], 48 * HEADS // 2)
            for j in range(4):
                sp.wait_ge(h_stored[j], 16 * (KC // 4))
            sp.dma_start(resid, h_scr).then_inc(h_loaded, 16)
            with sp.Fori(2, KC // 2) as q:
                load_out(q)

            with sp.Fori(0, NFB) as b:
                phase = (FF_T, b, T_FF)
                for k in range(4 * FB):
                    f, src = k // 4, (w_gate_v, w_up_v)[k % 4 // 2]
                    load(phase, k, src[:, TK * (k % 2):TK * (k % 2 + 1), bass.ds(b * FB * P + f * P, P)])
                for m in range(KC // 2):
                    load(phase, 4 * FB + m, w_down_v[:, bass.ds(b, 1), :, 2 * P * m:2 * P * (m + 1)]
                         .rearrange("p b k n -> p (b k) n"))

            for c in range(KC):
                s, f = c % 4, slice(c * P, (c + 1) * P)
                sp.wait_ge(y_left, c + 1)
                sp.wait_ge(y_right, c + 1)
                sp.dma_start(y_prompt[0][:, f].rearrange("(j p) n -> p j n", p=P), y_tok[:, s, 0:QB, :])\
                  .then_inc(y_stored[s], 16)
                sp.dma_start(y_sample[0][:, f], y_tok[0:TS, s, QB, :]).then_inc(y_stored[s], 16)
            for s in range(4):
                sp.wait_ge(y_stored[s], 32 * (KC // 4))

        @block.tensor
        def _(pe):
            acts = (act_hi, act_lo)
            hidden = (ff_hi, ff_lo)
            halves_of_tile = (list(range(TK // 2)), list(range(TK // 2, TK)))

            def chunk(phase, k, no, points, x_wait=None):
                if not known(no) or no >= 2:
                    pe.wait_ge(chunk_copied, no - 1)
                out = (acc if phase[0] == PAIR_T else acc_late)[(k // 2) % 2]
                for half in range(2):
                    pe.wait_ge(lo_ready, tile_no(phase, k + half) + 1)
                    for part in range(2):
                        for kk in halves_of_tile[part]:
                            if x_wait is not None:
                                pe.wait_ge(*x_wait(TK * half + kk))
                            mm = multiply((k + half) % SLOTS, TK, P, 0, *acts, TK * half, out, [kk],
                                          half == 0, half == 1)
                        if part == 0:
                            points[2 * half]()
                    mm.then_inc((first_used, chunk_done)[half], 1)
                    points[2 * half + 1]()

            def turn(out, src, n):
                return nc.tensor.transpose(out, src, ident[0:n, 0:n])

            pe.wait_ge(const_ready, 4)
            pe.wait_ge(cols_loaded, 16 * 8)
            turn(bank_d[:, 0:NCOL], col_rows, NCOL).then_inc(cols_turned, 1)
            for c in range(KC + 2):
                if c < KC:
                    if c >= 3:
                        pe.wait_ge(h_left, c - 2)
                        pe.wait_ge(h_right, c - 2)
                    if c == 2:
                        pe.wait_ge(cols_ready, 1)
                    for j in range(QB + 1):
                        if c in (0, KC // 2):
                            pe.wait_ge(x_loaded[j][c * 2 // KC], 32 if j in (0, QB) else 16)
                        n = P if j < QB else TAIL + TS
                        mm = turn(x_bank(c, j), x_tok[j][0:n, c * P:(c + 1) * P], n)
                    mm.then_inc(x_turned, 1)
                if c >= 2:
                    k = c - 2
                    if k % TK == 0:
                        pe.wait_ge(lo_ready, k // TK + 1)
                    pe.wait_ge(x_ready, k + 1)
                    mm = multiply(k // TK, TK, P, 0, act_hi, act_lo, k // TK * TK, acc[0], [k % TK],
                                  k < TK, k >= TK)
                    if k % TK == TK - 1:
                        mm.then_inc((first_used, chunk_done)[k // TK], 1)
            pe.wait_ge(h_left, KC)
            pe.wait_ge(h_right, KC)

            pe.wait_ge(diag_ready, 1)
            for j in range(QB + 1):
                n = P if j < QB else TAIL + TS
                mm = nc.tensor.matmul((bank_a, bank_b)[j // 4][:, j % 4 * P:j % 4 * P + n], neg1[0:n, :],
                                      buf_e[0:n, j * P:j * P + n], start=j % 4 == 0, stop=True,
                                      skip_group_check=True)
            mm.then_inc(ms_ready, 1)

            def row_sums(r):
                pe.wait_ge(sq_added, KC * r)
                for h, bank in enumerate((bank_a, bank_b)):
                    mm = nc.tensor.matmul(bank[:, 0:LHALF], neg1[:, :],
                                          buf_g[:, T - (2 - h) * LHALF:T - (1 - h) * LHALF],
                                          start=True, stop=True)
                mm.then_inc(ms_ready, 1)

            def into(out, w, x, start=False):
                return nc.tensor.matmul(out, w, x, start=start, stop=True, skip_group_check=True)

            def scores(a):
                pe.wait_ge(chunk_copied, 3 * a + 3)
                pe.wait_ge(kc_copied, a + 1)
                if known(a) and a == 0:
                    pe.wait_ge(bank_c_clear, 1)
                else:
                    pe.wait_ge(o_copied, a)
                into(bank_a[:, 0:512], kT[:, 0:P], qT[:, 0:MAIN], start=True)
                into(bank_b[:, 0:384], kT[:, P:2 * P], qT[:, P:MAIN], start=True)
                into(bank_b[:, 384:512], kT[:, 3 * P:4 * P], qT[:, 3 * P:MAIN])
                into(bank_c[:, 0:256], kT[:, 2 * P:3 * P], qT[:, 2 * P:MAIN], start=True)
                for j in range(QB):
                    at_c = BT - B2 + j * TAIL
                    into(bank_c[:, at_c:at_c + TAIL], kT[:, j * P:(j + 1) * P], qT[:, MAIN:TP])
                for j in range(2):
                    at_c = BC - B2 + j * TS
                    into(bank_c[:, at_c:at_c + TS], kcT[:, j * P:(j + 1) * P], qT[:, TP:T])
                into(bank_c[0:TAIL, BTT - B2:BNN - B2], kT[:, MAIN:TP], qT[:, MAIN:TP])
                into(bank_c[0:TS, BNN - B2:ZW - B2], kT[:, TP:T], qT[:, TP:T]).then_inc(z_ready, 1)

            def exponents(a):
                pe.wait_ge(sp_ready, a + 1)
                into(bank_a[:, 0:512], tri, relu[:, 0:512])
                into(bank_b[:, 0:512], tri, relu[:, 512:1024])
                into(bank_c[:, 0:BTT - B2], tri, relu[:, B2:BTT])
                into(bank_c[0:TAIL, BTT - B2:BNN - B2], tri[0:TAIL, 0:TAIL], relu[0:TAIL, BTT:BNN])
                into(bank_c[0:TS, BNN - B2:ZW - B2], tri[0:TS, 0:TS], relu[0:TS, BNN:ZW])

                def spread(at_c, n, blocks, w, x):
                    return into(bank_c[:, at_c:at_c + blocks * n].rearrange("p (b n) -> p b n", b=blocks), w,
                                x.unsqueeze(1).broadcast_to([x.shape[0], blocks, n]))
                for j in range(1, QB):
                    n = MAIN - j * P
                    later = relu[:, key_block_at[j]:key_block_at[j] + n]
                    for i in range(j):
                        end = key_block_at[i] % 512 + MAIN - i * P
                        into(score_banks[key_block_at[i] // 512][:, end - n:end], neg1[:, :], later)
                    spread(BT - B2, TAIL, j, neg1[:, :], relu[:, BT + j * TAIL:BT + (j + 1) * TAIL])
                spread(BT - B2, TAIL, QB, neg1[0:TAIL, :], relu[0:TAIL, BTT:BNN])
                spread(BC - B2, TS, 1, neg1[:, :], relu[:, BC + TS:BC + 2 * TS])
                spread(BC - B2, TS, 2, neg1[0:TS, :], relu[0:TS, BNN:ZW]).then_inc(e_ready, 1)

            def attend(a, par, bank_free):
                pe.wait_ge(w_ready, a + 1)
                pe.wait_ge(ends_copied, a + 1)
                pe.wait_ge(vc_loaded, 16 * (a + 1))
                pe.wait_ge(*bank_free)
                v = vtok[:, par]
                for j in range(QB):
                    n = MAIN - j * P
                    into(bank_d[:, j * P:MAIN], v[:, j, :], soft[:, key_block_at[j]:key_block_at[j] + n],
                         start=j == 0)
                for j in range(QB):
                    into(bank_c[:, 0:TAIL], v[:, j, :], soft[:, BT + j * TAIL:BT + (j + 1) * TAIL],
                         start=j == 0)
                into(bank_c[:, 0:TAIL], v[0:TAIL, QB, :], soft[0:TAIL, BTT:BNN])
                for j in range(2):
                    into(bank_c[:, TAIL:TAIL + TS], vc[:, j, :], soft[:, BC + j * TS:BC + (j + 1) * TS])
                into(bank_c[:, TAIL:TAIL + TS], v[0:TS, QB + 1, :], soft[0:TS, BNN:ZW]).then_inc(o_ready, 1)

            def norm_main(n, *bank_free):
                pe.wait_ge(sq_ready, n + 1)
                pe.wait_ge(*bank_free)
                into(bank_d[:, 0:MAIN], neg1[:, :], buf_e[:, 0:MAIN], start=True).then_inc(n1_ready, 1)

            def norm_ends(n, bank=None):
                if bank is None:
                    pe.wait_ge(n1_log, n + 1)
                    bank = bank_d
                into(bank[:, 256:256 + T - MAIN], neg1[:, :], buf_e[:, MAIN:T], start=True)\
                    .then_inc(n2_ready, 1)

            def turn_cache(i, *bank_free):
                pe.wait_ge(kc_loaded, 16 * (i + 1))
                pe.wait_ge(*bank_free)
                for j in range(2):
                    mm = turn(bank_d[:, j * P:(j + 1) * P], kc_tok[:, j, :], P)
                mm.then_inc(kc_turned, 1)

            def turn_main(src, done, copied, bank_free):
                pe.wait_ge(*copied)
                pe.wait_ge(*bank_free)
                for j in range(QB):
                    mm = turn(bank_d[:, j * P:(j + 1) * P], src[:, j * P:(j + 1) * P], P)
                mm.then_inc(done, 1)

            def turn_ends(i):
                pe.wait_ge(k_copied, i + 1)
                for j, src in enumerate((vT, kT)):
                    turn(bank_d[0:TAIL, j * P:(j + 1) * P], src[:, MAIN:TP], P)
                    mm = turn(bank_d[0:TS, (2 + j) * P:(3 + j) * P], src[:, TP:T], P)
                mm.then_inc(ends_turned, 1)

            def walk(p, u, i, at_point, begin=0):
                for c in range(begin, 3):
                    points = [at_point.get(4 * c + m, lambda: None) for m in range(1, 5)]
                    chunk((PAIR_T, p, 0), 6 * u + 2 * c, 3 * i + c, points)

            def head(p, u, i, has_attention, has_norm):
                a, n = i - 1, i - 2

                def after_first_tile():
                    if has_attention:
                        scores(a)
                    if has_norm:
                        norm_main(n, ends_copied, i)

                def after_v():
                    if has_norm:
                        norm_ends(n)
                        pe.wait_ge(n2_log, n + 1)
                    turn_cache(i, *((ends_copied, i) if has_attention else (cols_ready, 1)))

                at_point = {
                    2: after_first_tile,
                    4: after_v,
                    6: lambda: turn_main(vT, v_turned, (chunk_copied, 3 * i + 1), (kc_copied, i + 1)),
                    11: lambda: turn_main(kT, k_turned, (chunk_copied, 3 * i + 2),
                                          (o_copied, i) if has_attention else (v_copied, i + 1)),
                }
                if has_attention:
                    at_point[1] = lambda: turn_ends(a)
                    at_point[7] = lambda: exponents(a)
                    at_point[9] = lambda: attend(a, (u + 1) % 2, (v_copied, i + 1))
                if not known(i) or i > 0:
                    walk(p, u, i, at_point)
                else:
                    after_v()
                    walk(p, u, i, at_point, begin=1)

            def group(p, u, i, first_pair=False):
                last = HEADS - 1
                if first_pair and u == 0:
                    def after_first_tile():
                        scores(last)
                        norm_main(last - 1, ends_copied, HEADS)
                    at_point = {1: lambda: turn_ends(last), 2: after_first_tile,
                                4: lambda: norm_ends(last - 1), 7: lambda: exponents(last),
                                9: lambda: attend(last, last % 2, (n2_log, last))}
                else:
                    at_point = {6: lambda: norm_main(i - 1, n2_log, i - 1), 8: lambda: norm_ends(i - 1)}
                    if first_pair:
                        at_point[2] = lambda: norm_main(last, o_copied, HEADS)
                        at_point[4] = lambda: norm_ends(last)
                walk(p, u, i, at_point)

            for u in range(2):
                head(0, u, u, u > 0, False)
            with pe.Fori(1, HEADS // 2) as p:
                for u in range(2):
                    head(p, u, 2 * p + u, True, True)
            for u in range(2):
                group(HEADS // 2, u, HEADS + u, first_pair=True)
            with pe.Fori(HEADS // 2 + 1, (HEADS + GROUPS) // 2) as p:
                for u in range(2):
                    group(p, u, 2 * p + u)

            no_points = [lambda: None] * 4

            def last_norm_and_rows():
                norm_main(HEADS + GROUPS - 1, n2_log, HEADS + GROUPS - 1)
                norm_ends(HEADS + GROUPS - 1, bank_c)
                pe.wait_ge(u_ends, GROUPS)
                turn(bank_a[0:4 * GROUPS, 0:P], ulast_f, P).then_inc(ulast_turned, 1)

            def mix_chunk(c):
                return mix_split[c // TK], c % TK + 1

            for c in range(2):
                chunk((4, 0, T_OUT), 2 * c, CH_OUT + c,
                      [lambda: None, last_norm_and_rows] + no_points[2:] if c == 0 else no_points,
                      mix_chunk if c == 0 else None)
            with pe.Fori(1, KC // 2) as q:
                for c in range(2):
                    chunk((4, q, T_OUT), 2 * c, 2 * q + CH_OUT + c, no_points)
            row_sums(1)

            def ffn_block(b, first):
                phase = (FF_T, b, T_FF)
                ch = b * FF_CH + CH_FF
                for j in range(2 * FB):
                    begins = first and j == 0
                    chunk(phase, 2 * j, ch + j,
                          no_points[:3] + [lambda: row_sums(2)] if begins else no_points,
                          (lambda c: (f_split, c + 1)) if begins else None)
                for m in range(KC // 2):
                    k = 4 * FB + m
                    pe.wait_ge(lo_ready, tile_no(phase, k) + 1)
                    for o in range(2):
                        no = ch + 2 * FB + 2 * m + o
                        pe.wait_ge(chunk_copied, no - 1)
                        for kk in range(FB):
                            if m == 0 and o == 0:
                                pe.wait_ge(ff_ready, b * FB + kk + 1)
                            mm = multiply(k % SLOTS, FB, P, o * P, *hidden, 0, acc_late[o], [kk],
                                          True, True)
                        mm.then_inc(chunk_done, 1)

            ffn_block(0, True)
            with pe.Fori(1, NFB) as b:
                ffn_block(b, False)

            row_sums(3)
            for c in range(KC):
                s = c % 4
                pe.wait_ge(y_ready, c + 1)
                if c >= 4:
                    pe.wait_ge(y_left, c - 3)
                    pe.wait_ge(y_right, c - 3)
                for j in range(QB + 1):
                    n = P if j < QB else TS
                    at_t = NMETA + j * P
                    mm = turn(ps[0:n, 2 * s + j // 3, (j % 3) * P:(j % 3 + 1) * P],
                              resid[:, c, at_t:at_t + n], P)
                mm.then_inc(y_turned, 1)

        @block.scalar
        def _(act):
            A = nc.scalar.activation
            kp = new_k_prompt[0, 0].rearrange("t h d -> h t d")
            vp = new_v_prompt[0, 0].rearrange("t h d -> h t d")
            ks = new_k_sample[0, 0].rearrange("t h d -> h t d")
            vs = new_v_sample[0, 0].rearrange("t h d -> h t d")
            kc_v = cache_k[0, 0].rearrange("(j p) h d -> p j h d", p=P)
            vc_v = cache_v[0, 0].rearrange("(j p) h d -> p j h d", p=P)

            def load_cache(cache, i, dst, done):
                act.dma_start(dst, cache[:, :, bass.ds(i, 1), :].rearrange("p j h d -> p (j h) d"))\
                   .then_inc(done, 16)

            def store_head(prompt, sample, i, src, done):
                act.dma_start(prompt[bass.ds(i, 1), 0:MAIN, :].rearrange("h (j p) d -> p (h j) d", p=P),
                              src[:, 0:QB, :]).then_inc(done, 16)
                act.dma_start(prompt[bass.ds(i, 1), MAIN:TP, :].rearrange("h p d -> p (h d)"),
                              src[0:TAIL, QB, :]).then_inc(done, 16)
                act.dma_start(sample[bass.ds(i, 1), :, :].rearrange("h p d -> p (h d)"),
                              src[0:TS, QB + 1, :]).then_inc(done, 16)

            def make_rstd(r):
                act.wait_ge(ms_ready, r + 1)
                out = rstd[:, LATE if r else slice(0, T)]
                if r:
                    A(out.rearrange("p (h t) -> p h t", h=2), ps[:, 4:6, 0:LHALF], ACT.Ln,
                      scale=-1.0 / D, bias=eps[:, 0:1]).then_inc(ms_log, 1)
                else:
                    A(out[:, 0:MAIN], bank_a[:, 0:MAIN], ACT.Ln, scale=-1.0 / D, bias=eps[:, 0:1])
                    A(out[:, MAIN:T], bank_b[:, 0:T - MAIN], ACT.Ln, scale=-1.0 / D, bias=eps[:, 0:1])\
                        .then_inc(ms_log, 1)
                act.wait_ge(ms_log, r + 1)
                A(out, out, ACT.Exp, scale=-0.5).then_inc(rstd_ready, 1)

            def norm_log_main(n):
                act.wait_ge(n1_ready, n + 1)
                A(buf_e[:, 0:MAIN], bank_d[:, 0:MAIN], ACT.Ln, scale=-1.0 / P, bias=eps[:, 0:1])\
                    .then_inc(n1_log, 1)

            def norm_finish(n, bank=bank_d):
                act.wait_ge(n2_ready, n + 1)
                A(buf_e[:, MAIN:T], bank[:, 256:256 + T - MAIN], ACT.Ln, scale=-1.0 / P, bias=eps[:, 0:1])\
                    .then_inc(n2_log, 1)
                act.wait_ge(n2_log, n + 1)
                A(buf_e[:, :], buf_e[:, :], ACT.Exp, scale=-0.5).then_inc(norm_ready, 1)

            parts = ((bank_a, 0, 512), (bank_b, 512, 512), (bank_c, B2, ZW - B2))

            def soft_begin(a):
                act.wait_ge(z_ready, a + 1)
                for bank, at_z, n in parts:
                    A(soft[:, at_z:at_z + n], bank[:, 0:n], ACT.Abs)
                for bank, at_z, n in parts:
                    last = A(relu[:, at_z:at_z + n], bank[:, 0:n], ACT.Relu)
                last.then_inc(abs_ready, 1)

            def soft_finish(a):
                act.wait_ge(abs_ready, a + 1)
                A(soft, soft, ACT.Exp, scale=-1.0).then_inc(exp_ready, 1)
                act.wait_ge(exp_ready, a + 1)
                A(soft, soft, ACT.Ln, bias=1.0).then_inc(log_ready, 1)

            def weights_of(a):
                act.wait_ge(e_ready, a + 1)
                for bank, at_z, n in parts:
                    last = A(soft[:, at_z:at_z + n], bank[:, 0:n], ACT.Exp)
                last.then_inc(w_made, 1)

            def square_mix(src, n, ready):
                act.wait_ge(*ready)
                if not known(n) or n > 0:
                    act.wait_ge(mixed, n)
                A(buf_e[:, :], src, ACT.Square).then_inc(sq_ready, 1)

            def square_row(src, r, c, buf_free=None, before=None):
                if buf_free is not None:
                    act.wait_ge(*buf_free)
                act.wait_ge(sq_added, KC * (r - 1) + c if before is None else before)
                A(buf_e[:, LATE], src, ACT.Square).then_inc(sq_made, 1)

            for at_col, rows in ((C_STATE, state_conv[0, 0]), (C_CONVW, conv_w[0]),
                                 (C_PREMIX, g_pre_mix), (C_POSTMIX, g_post_mix),
                                 (C_ATTN, g_attn_out), (C_CONV, g_conv_out),
                                 (C_PREFFN, g_pre_ffn), (C_POSTFFN, g_post_ffn)):
                rows = rows.rearrange("a (g p) -> (a g) p", p=P)
                act.dma_start(col_rows[at_col:at_col + rows.shape[0], :], rows).then_inc(cols_loaded, 16)

            def square_x(h, j):
                n = P if j < QB else TAIL + TS
                k = (QB + 1) * h + j
                act.wait_ge(x_loaded[j][h], 32 if j in (0, QB) else 16)
                if k >= 2:
                    act.wait_ge(x_squared, k - 1)
                A(squares_out[0:n, k % 2, :],
                  x_tok[j][0:n, h * D // 2:(h + 1) * D // 2], ACT.Square,
                  accum_out=sq_sums[0:n, h, j:j + 1]).then_inc(x_squared, 1)

            act.wait_ge(const_ready, 4)
            for j in range(QB + 1):
                square_x(0, j)
            round_weights((PAIR_T, 0, 0), 0)

            def copy_right(c):
                act.wait_ge(x_turned, c + 1)
                if c >= 4:
                    act.wait_ge(h_stored[c % 4], 16 * (c // 4))
                    act.wait_ge(x_ready, c - 3)
                A(h_ring[:, c % 4, 3 * P:T], ps[:, 3 + 2 * (c % 3), 0:T - 3 * P], ACT.Copy)\
                    .then_inc(h_right, 1)

            copy_right(0)
            for c in range(KC):
                s = c % 4
                if c + 1 < KC:
                    copy_right(c + 1)
                if c == 0:
                    act.wait_ge(cols_ready, 1)
                act.wait_ge(h_left, c + 1)
                act.wait_ge(h_right, c + 1)
                A(act_hi[:, c, :], h_ring[:, s, :], ACT.Copy, scale=cols[:, C_PREMIX + c:C_PREMIX + c + 1])\
                    .then_inc(x_hi_ready, 1)
                if 1 <= c <= QB + 1:
                    square_x(1, c - 1)
                if c in (6, 12):
                    round_weights((PAIR_T, 0, 0), c // 6)

            def head(p, u, i, has_attention, has_norm):
                a, n = i - 1, i - 2
                for s in range(6):
                    round_weights((PAIR_T, p, 0), 6 * u + s + LEAD)
                    if s == 0:
                        if has_attention:
                            act.wait_ge(kc_turned, i)
                        load_cache(kc_v, i, kc_tok, kc_loaded)
                        if has_norm:
                            norm_log_main(n)
                        if has_attention:
                            soft_begin(a)
                    if s == 1:
                        if not has_attention:
                            make_rstd(0)
                        if has_norm:
                            norm_finish(n)
                        if has_attention:
                            soft_finish(a)
                            act.wait_ge(ends_copied, a + 1)
                            store_head(kp, ks, a, ktok, k_stored)
                            store_head(vp, vs, a, vtok[:, (u + 1) % 2], v_stored[(u + 1) % 2])
                    if s == 3 and has_attention:
                        weights_of(a)
                    if s == 4:
                        if has_attention:
                            square_mix(buf_g[:, :], a, (o_copied, a + 1))
                            act.wait_ge(o_ready, i)
                        load_cache(vc_v, i, vc, vc_loaded)

            def group(p, u, i, first_pair=False):
                last = HEADS - 1
                for s in range(6):
                    round_weights((PAIR_T, p, 0), 6 * u + s + LEAD)
                    if first_pair and u == 0:
                        if s == 0:
                            norm_log_main(last - 1)
                            soft_begin(last)
                        if s == 1:
                            norm_finish(last - 1)
                            soft_finish(last)
                            act.wait_ge(ends_copied, HEADS)
                            store_head(kp, ks, last, ktok, k_stored)
                            store_head(vp, vs, last, vtok[:, last % 2], v_stored[last % 2])
                        if s == 3:
                            weights_of(last)
                        if s == 4:
                            square_mix(buf_g[:, :], last, (o_copied, HEADS))
                        continue
                    if first_pair and s == 0:
                        norm_log_main(last)
                    if s == 1:
                        if first_pair:
                            norm_finish(last)
                        square_mix(vT[:, 0:T], i - 1, (conv_step, 4 * (i - HEADS)))
                    if s == 2:
                        norm_log_main(i - 1)
                    if s == 3:
                        norm_finish(i - 1)

            for u in range(2):
                head(0, u, u, u > 0, False)
            with act.Fori(1, HEADS // 2) as p:
                for u in range(2):
                    head(p, u, 2 * p + u, True, True)
            for u in range(2):
                group(HEADS // 2, u, HEADS + u, first_pair=True)
            with act.Fori(HEADS // 2 + 1, (HEADS + GROUPS) // 2) as p:
                for u in range(2):
                    group(p, u, 2 * p + u)

            def mix_high(c):
                act.wait_ge(mixed, c + 1)
                nc.scalar.copy(act_hi[:, c, LATE], wide_c[:, c, LATE]).then_inc(mix_hi, 1)

            end = HEADS + GROUPS
            act.wait_ge(chunk_done, 3 * end)
            for c in range(6):
                mix_high(c)
            round_weights((4, 0, T_OUT), LEAD)
            square_mix(vT[:, 0:T], end - 1, (conv_step, 4 * GROUPS))
            for c in range(6, 12):
                mix_high(c)
            norm_log_main(end - 1)
            norm_finish(end - 1, bank_c)
            round_weights((4, 0, T_OUT), LEAD + 1)
            for c in range(12, KC):
                mix_high(c)
            act.wait_ge(ulast_copied, 1)
            rows = relu[0:4 * GROUPS, 0:P]
            act.dma_start(new_conv_prompt[0, 0].rearrange("a (g p) -> (a g) p", p=P), rows[0:2 * GROUPS, :])\
               .then_inc(conv_stored, 16)
            act.dma_start(new_conv_sample[0, 0].rearrange("a (g p) -> (a g) p", p=P),
                          rows[2 * GROUPS:4 * GROUPS, :]).then_inc(conv_stored, 16)

            def out_round(q, k_from):
                for k in range(4):
                    if k >= k_from:
                        round_weights((4, q, T_OUT), k + LEAD)
                    if k % 2:
                        c = 2 * q + k // 2
                        act.wait_ge(chunk_copied, c + CH_OUT + 1)
                        square_row(wide_c[:, bass.ds(c, 1), LATE].rearrange("p c t -> p (c t)"), 1, c,
                                   (mixed, HEADS + GROUPS))
            out_round(0, 2)
            with act.Fori(1, KC // 2) as q:
                out_round(q, 0)

            make_rstd(1)
            with act.Fori(KC, 2 * KC) as squares:
                c = squares - KC
                h = resid[:, bass.ds(c, 1), LATE]
                act.wait_ge(chunk_done, CH_FF)
                act.wait_ge(h2_ready, c + 1)
                A(act_hi[:, bass.ds(c, 1), LATE], h, ACT.Copy, scale=cols[:, bass.ds(c + C_PREFFN, 1)])\
                    .then_inc(f_hi, 1)
                square_row(h.rearrange("p c t -> p (c t)"), 2, c, (ms_ready, 2), squares)
            make_rstd(2)

            def ffn_block(b, last):
                phase = (FF_T, b, T_FF)
                ch = b * FF_CH + CH_FF
                for k in range(FF_T):
                    if not last or k + LEAD < FF_T:
                        round_weights(phase, k + LEAD)
                    f = k // 4
                    if f < FB and k % 4 == 1:
                        act.wait_ge(chunk_copied, ch + 2 * f + 1)
                        A(buf_e[:, LATE], buf_g[:, LATE], ACT.Exp, scale=-1.0).then_inc(e_neg, 1)
                    if f < FB and k % 4 == 3:
                        act.wait_ge(chunk_copied, ch + 2 * f + 2)
                        nc.scalar.copy(ff_hi[:, f, LATE], buf_g[:, LATE]).then_inc(ff_hi_ready, 1)
                    if last and f >= FB:
                        for c in (2 * (k - 4 * FB), 2 * (k - 4 * FB) + 1):
                            act.wait_ge(chunk_copied, ch + 2 * FB + c + 1)
                            square_row(wide_c[:, c, LATE], 3, c)

            with act.Fori(0, NFB - 1) as b:
                ffn_block(b, False)
            ffn_block(NFB - 1, True)

            make_rstd(3)
            for c in range(KC):
                s = c % 4
                act.wait_ge(y_turned, c + 1)
                if c >= 4:
                    act.wait_ge(y_stored[s], 32 * (c // 4))
                A(y_tok[:, s, 3, :], ps[:, 2 * s + 1, 0:P], ACT.Copy)
                A(y_tok[0:TS, s, QB, :], ps[0:TS, 2 * s + 1, P:2 * P], ACT.Copy)\
                    .then_inc(y_right, 1)

        @block.vector
        def _(dve):
            V = nc.vector

            def column(at_col):
                return cols[:, bass.ds(at_col, 1)] if not known(at_col) else cols[:, at_col:at_col + 1]

            def in_halves(x):
                return x.rearrange("p (h t) -> p h t", h=2)

            def copy_chunk(no, par, out, scale=None):
                dve.wait_ge(chunk_done, no + 1)
                if scale is None:
                    ins = V.tensor_tensor(in_halves(out[:, 0:T]), acc[par], in_halves(rstd[:, :]), ALU.mult)
                else:
                    ins = V.scalar_tensor_tensor(out=in_halves(out[:, 0:T]), in0=acc[par], scalar=scale,
                                                 in1=in_halves(rstd[:, :]), op0=ALU.mult, op1=ALU.mult)
                ins.then_inc(chunk_copied, 1)

            def mix(n, src, at_col):
                dve.wait_ge(norm_ready, n + 1)
                out = wide_c[:, bass.ds(n, 1), :].rearrange("p c t -> p (c t)")
                V.scalar_tensor_tensor(out=out, in0=src, scalar=column(at_col), in1=buf_e[:, :],
                                       op0=ALU.mult, op1=ALU.mult).then_inc(mixed, 1)

            def ends(a, par):
                dve.wait_ge(ends_turned, a + 1)
                V.tensor_copy(vtok[0:TAIL, par, QB, :], bank_d[0:TAIL, 0:P])
                V.tensor_copy(ktok[0:TAIL, QB, :], bank_d[0:TAIL, P:2 * P])
                V.tensor_copy(vtok[0:TS, par, QB + 1, :], bank_d[0:TS, 2 * P:3 * P])
                V.tensor_copy(ktok[0:TS, QB + 1, :], bank_d[0:TS, 3 * P:4 * P]).then_inc(ends_copied, 1)

            def softplus(a):
                dve.wait_ge(log_ready, a + 1)
                V.tensor_tensor(relu, relu, soft, ALU.add).then_inc(sp_made, 1)

            def outputs(a):
                dve.wait_ge(o_ready, a + 1)
                V.tensor_copy(buf_g[:, 0:MAIN], bank_d[:, 0:MAIN])
                V.tensor_copy(buf_g[:, MAIN:T], bank_c[:, 0:T - MAIN]).then_inc(o_copied, 1)

            def conv(g):
                dve.wait_ge(u_ends, g + 1)
                taps = [column(g + C_CONVW + GROUPS * j) for j in range(3)]
                for j in range(3):
                    if j:
                        dve.wait_ge(conv_step, 4 * g + j)
                    for to, n, at_u in ((0, TP, 0), (TP, TS, TP + 2)):
                        x = uext[:, at_u + j:at_u + j + n]
                        if j == 0:
                            last = V.tensor_scalar(vT[:, to:to + n], x, taps[0], None, ALU.mult)
                        else:
                            last = V.scalar_tensor_tensor(out=vT[:, to:to + n], in0=x, scalar=taps[j],
                                                          in1=vT[:, to:to + n], op0=ALU.mult, op1=ALU.add)
                    last.then_inc(conv_step, 1)
                dve.wait_ge(conv_step, 4 * g + 3)
                V.tensor_tensor(vT[:, 0:T], vT[:, 0:T], qT[:, 0:T], ALU.mult).then_inc(conv_step, 1)

            def conv_input(no, par, g):
                dve.wait_ge(chunk_done, no + 1)
                dve.wait_ge(c_scaled, g + 1)
                V.tensor_tensor(uext[:, 2:2 + HALF], acc[par][:, 0, :], kT[:, 0:HALF], ALU.mult)
                V.tensor_tensor(uext[:, 2 + HALF:2 + TP], acc[par][:, 1, 0:TP - HALF], kT[:, HALF:TP], ALU.mult)
                V.tensor_tensor(uext[:, 4 + TP:4 + T], acc[par][:, 1, TP - HALF:HALF], kT[:, TP:T],
                                ALU.mult).then_inc(chunk_copied, 1)
                state = cols[:, C_STATE:C_STATE + 2 * GROUPS].rearrange("p (a g) -> p a g", a=2)
                V.tensor_copy(uext[:, 2 + TP:4 + TP].unsqueeze(2), state[:, :, bass.ds(g, 1)])
                dve.wait_ge(chunk_copied, no + 1)
                V.tensor_copy(ulast[:, 0:2, bass.ds(g, 1)], uext[:, TP:2 + TP].unsqueeze(2))
                V.tensor_copy(ulast[:, 2:4, bass.ds(g, 1)], uext[:, 2 + T:4 + T].unsqueeze(2))\
                    .then_inc(u_ends, 1)

            V.memset(eps[:, :], EPS)
            V.memset(sq_sums[:, :, :], 0.0).then_inc(const_ready, 1)
            dve.wait_ge(cols_turned, 1)
            V.tensor_copy(cols[:, :], bank_d[:, 0:NCOL]).then_inc(cols_ready, 1)
            rest_of_weights((PAIR_T, 0, 0), 0)
            dve.wait_ge(cols_ready, 1)

            def copy_left(c):
                dve.wait_ge(x_turned, c + 1)
                if c >= 4:
                    dve.wait_ge(h_stored[c % 4], 16 * (c // 4))
                V.tensor_copy(h_ring[:, c % 4, 0:3 * P], ps[:, 2 + 2 * (c % 3), 0:3 * P]).then_inc(h_left, 1)

            copy_left(0)
            for c in range(KC):
                s = c % 4
                if c + 1 < KC:
                    copy_left(c + 1)
                dve.wait_ge(x_hi_ready, c + 1)
                V.scalar_tensor_tensor(out=act_lo[:, c, :], in0=h_ring[:, s, :], scalar=column(C_PREMIX + c),
                                       in1=act_hi[:, c, :].bitcast(F32), op0=ALU.mult,
                                       op1=ALU.subtract).then_inc(x_ready, 1)
                if c in (6, 12):
                    rest_of_weights((PAIR_T, 0, 0), c // 6)
                if c == 10:
                    dve.wait_ge(x_squared, 2 * (QB + 1))
                    V.tensor_tensor(sq_sums[:, 0, :], sq_sums[:, 0, :], sq_sums[:, 1, :], ALU.add)\
                        .then_inc(x_summed, 1)
                    dve.wait_ge(x_summed, 1)
                    for j in range(QB + 1):
                        n = P if j < QB else TAIL + TS
                        ins = V.tensor_scalar(buf_e[0:n, j * P:j * P + n], ident[0:n, 0:n],
                                              sq_sums[0:n, 0, j:j + 1], None, ALU.mult)
                    ins.then_inc(diag_ready, 1)
            dve.wait_ge(h_right, KC)
            dve.wait_ge(h_left, KC)
            V.memset(bank_c[:, BTT - B2:ZW - B2], 0.0).then_inc(bank_c_clear, 1)
            for j in range(4):
                dve.wait_ge(h_stored[j], 16 * (KC // 4))
            V.memset(uext[:, 0:2], 0.0)

            def head(p, u, i, has_attention, has_norm):
                a, n = i - 1, i - 2
                no = 3 * i
                for s in range(6):
                    rest_of_weights((PAIR_T, p, 0), 6 * u + s + LEAD)
                    if s == 0 and has_attention:
                        ends(a, (u + 1) % 2)
                    if s == 1:
                        if not has_attention:
                            dve.wait_ge(rstd_ready, 1)
                        copy_chunk(no, (3 * u) % 2, vT)
                        dve.wait_ge(kc_turned, i + 1)
                        V.tensor_copy(kcT, bank_d[:, 0:2 * P]).then_inc(kc_copied, 1)
                        if has_norm:
                            mix(n, buf_g[:, :], n + C_ATTN)
                        if has_attention:
                            softplus(a)
                    if s == 2:
                        dve.wait_ge(v_turned, i + 1)
                        if has_norm:
                            dve.wait_ge(v_stored[u], 48 * p)
                        V.tensor_copy(vtok[:, u, 0:QB, :], bank_d.rearrange("p (j d) -> p j d", d=P))\
                            .then_inc(v_copied, 1)
                    if s == 3:
                        copy_chunk(no + 1, (3 * u + 1) % 2, kT)
                    if s == 4 and has_attention:
                        outputs(a)
                    if s == 5:
                        copy_chunk(no + 2, (3 * u + 2) % 2, qT, SCALE)
                        dve.wait_ge(k_turned, i + 1)
                        if has_attention:
                            dve.wait_ge(k_stored, 48 * i)
                        V.tensor_copy(ktok[:, 0:QB, :], bank_d.rearrange("p (j d) -> p j d", d=P))\
                            .then_inc(k_copied, 1)

            def group(p, u, i, first_pair=False):
                last, g, no = HEADS - 1, i - HEADS, 3 * i
                begins = first_pair and u == 0
                for s in range(6):
                    rest_of_weights((PAIR_T, p, 0), 6 * u + s + LEAD)
                    if s == 0:
                        if begins:
                            ends(last, last % 2)
                        else:
                            conv(g - 1)
                    if s == 1:
                        if not begins:
                            dve.wait_ge(conv_step, 4 * g)
                        copy_chunk(no, (3 * u) % 2, qT)
                        if begins:
                            mix(last - 1, buf_g[:, :], C_ATTN + last - 1)
                            softplus(last)
                        elif first_pair:
                            mix(last, buf_g[:, :], C_ATTN + last)
                    if s == 3:
                        copy_chunk(no + 1, (3 * u + 1) % 2, kT)
                        dve.wait_ge(chunk_copied, no + 2)
                        V.tensor_tensor(kT[:, 0:T], kT[:, 0:T], rstd[:, :], ALU.mult).then_inc(c_scaled, 1)
                    if s == 4:
                        if begins:
                            outputs(last)
                        else:
                            mix(i - 1, vT[:, 0:T], g - 1 + C_CONV)
                    if s == 5:
                        conv_input(no + 2, (3 * u + 2) % 2, g)

            for u in range(2):
                head(0, u, u, u > 0, False)
            with dve.Fori(1, HEADS // 2) as p:
                for u in range(2):
                    head(p, u, 2 * p + u, True, True)
            for u in range(2):
                group(HEADS // 2, u, HEADS + u, first_pair=True)
            with dve.Fori(HEADS // 2 + 1, (HEADS + GROUPS) // 2) as p:
                for u in range(2):
                    group(p, u, 2 * p + u)

            def mix_rest(c):
                dve.wait_ge(mix_hi, c + 1)
                V.tensor_tensor(act_lo[:, c, LATE], wide_c[:, c, LATE], act_hi[:, c, LATE].bitcast(F32),
                                ALU.subtract).then_inc(mix_split[1], 1)

            rest_of_weights((4, 0, T_OUT), LEAD)
            conv(GROUPS - 1)
            for c in range(TK, 12):
                mix_rest(c)
            rest_of_weights((4, 0, T_OUT), LEAD + 1)
            mix(HEADS + GROUPS - 1, vT[:, 0:T], C_CONV + GROUPS - 1)
            for c in range(12, KC):
                mix_rest(c)
            dve.wait_ge(ulast_turned, 1)
            V.tensor_copy(relu[0:4 * GROUPS, 0:P], bank_a[0:4 * GROUPS, 0:P]).then_inc(ulast_copied, 1)

            def out_round(q, k_from):
                for k in range(4):
                    if k >= k_from:
                        rest_of_weights((4, q, T_OUT), k + LEAD)
                    if k % 2:
                        c = 2 * q + k // 2
                        dve.wait_ge(chunk_done, c + CH_OUT + 1)
                        out = wide_c[:, bass.ds(c, 1), LATE].rearrange("p c t -> p (c t)")
                        V.tensor_copy(in_halves(out), acc_late[k // 2]).then_inc(chunk_copied, 1)
            out_round(0, 2)
            with dve.Fori(1, KC // 2) as q:
                out_round(q, 0)

            def scale_row(c, done):
                x = wide_c[:, bass.ds(c, 1), LATE].rearrange("p c t -> p (c t)")
                g = column(c + (C_POSTMIX if done is scaled else C_POSTFFN))
                V.scalar_tensor_tensor(out=x, in0=x, scalar=g, in1=rstd[:, LATE], op0=ALU.mult,
                                       op1=ALU.mult).then_inc(done, 1)

            def split_row(c):
                dve.wait_ge(f_hi, c + 1)
                V.scalar_tensor_tensor(out=act_lo[:, bass.ds(c, 1), LATE].rearrange("p c t -> p (c t)"),
                                       in0=resid[:, bass.ds(c, 1), LATE].rearrange("p c t -> p (c t)"),
                                       scalar=column(c + C_PREFFN),
                                       in1=act_hi[:, bass.ds(c, 1), LATE].rearrange("p c t -> p (c t)").bitcast(F32),
                                       op0=ALU.mult, op1=ALU.subtract).then_inc(f_split, 1)
            dve.wait_ge(rstd_ready, 2)
            for c in range(2):
                scale_row(c, scaled)
            with dve.Fori(0, KC - 2) as c:
                scale_row(c + 2, scaled)
                split_row(c)
            for c in range(KC - 2, KC):
                split_row(c)

            gate, sigmoid, one_over_rms = buf_g[:, LATE], buf_e[:, LATE], rstd[:, LATE]

            def ffn_block(b, first, last):
                phase = (FF_T, b, T_FF)
                ch = b * FF_CH + CH_FF
                for k in range(FF_T):
                    if not last or k + LEAD < FF_T:
                        rest_of_weights(phase, k + LEAD)
                    f = k // 4
                    if f < FB:
                        if k % 4 == 1:
                            if first and f == 0:
                                dve.wait_ge(rstd_ready, 3)
                            else:
                                dve.wait_ge(ff_ready, b * FB + f)
                            dve.wait_ge(chunk_done, ch + 2 * f + 1)
                            V.tensor_tensor(in_halves(gate), acc_late[0], in_halves(one_over_rms), ALU.mult)\
                                .then_inc(chunk_copied, 1)
                        step = b * 4 * FB + 4 * f
                        if k % 4 == 2:
                            dve.wait_ge(e_neg, b * FB + f + 1)
                            V.tensor_scalar(sigmoid, sigmoid, 1.0, None, ALU.add).then_inc(ff_step, 1)
                            dve.wait_ge(ff_step, step + 1)
                            V.reciprocal(sigmoid, sigmoid).then_inc(ff_step, 1)
                            dve.wait_ge(ff_step, step + 2)
                            V.tensor_tensor(gate, gate, sigmoid, ALU.mult).then_inc(ff_step, 1)
                            dve.wait_ge(ff_step, step + 3)
                            V.tensor_tensor(gate, gate, one_over_rms, ALU.mult).then_inc(ff_step, 1)
                        if k % 4 == 3:
                            dve.wait_ge(ff_step, step + 4)
                            dve.wait_ge(chunk_done, ch + 2 * f + 2)
                            V.tensor_tensor(in_halves(gate), acc_late[1], in_halves(gate), ALU.mult)\
                                .then_inc(chunk_copied, 1)
                            dve.wait_ge(ff_hi_ready, b * FB + f + 1)
                            V.tensor_tensor(ff_lo[:, f, LATE], gate, ff_hi[:, f, LATE].bitcast(F32),
                                            ALU.subtract).then_inc(ff_ready, 1)
                    else:
                        for o in range(2):
                            c = 2 * (k - 4 * FB) + o
                            dve.wait_ge(chunk_done, ch + 2 * FB + c + 1)
                            y = in_halves(wide_c[:, c, LATE])
                            ins = V.tensor_copy(y, acc_late[o]) if first else V.tensor_tensor(y, acc_late[o], y, ALU.add)
                            ins.then_inc(chunk_copied, 1)

            ffn_block(0, True, False)
            with dve.Fori(1, NFB - 1) as b:
                ffn_block(b, False, False)
            ffn_block(NFB - 1, False, True)

            dve.wait_ge(rstd_ready, 4)
            for c in range(3):
                scale_row(c, y_scaled)
            for c in range(KC):
                if c + 3 < KC:
                    scale_row(c + 3, y_scaled)
                s = c % 4
                dve.wait_ge(y_turned, c + 1)
                if c >= 4:
                    dve.wait_ge(y_stored[s], 32 * (c // 4))
                V.tensor_copy(y_tok[:, s, 0:3, :], ps[:, 2 * s, 0:3 * P].rearrange("p (j f) -> p j f", f=P))\
                    .then_inc(y_left, 1)

        def add_square(pool, r, c):
            total, square = buf_g[:, LATE], buf_e[:, LATE]
            if c == 0:
                ins = nc.gpsimd.tensor_copy(total, square)
            else:
                pool.wait_ge(sq_added, KC * (r - 1) + c)
                ins = nc.gpsimd.tensor_tensor(total, total, square, ALU.add)
            ins.then_inc(sq_added, 1)

        @block.gpsimd
        def _(pool):
            G = nc.gpsimd
            G.memset(neg1[:, :], -1.0).then_inc(const_ready, 1)
            G.memset(ident[:, :], 0.0).then_inc(pool_step, 1)
            pool.wait_ge(pool_step, 1)
            G.affine_select(out=ident[:, :], in_=ident[:, :], compare_op=ALU.not_equal, fill=1.0, base=0,
                            pattern=[[-1, P]], channel_multiplier=1).then_inc(const_ready, 1)
            pool.wait_ge(const_ready, 3)
            G.affine_select(out=tri, in_=neg1[:, :], compare_op=ALU.is_ge, fill=0.0, base=0,
                            pattern=[[-1, P]], channel_multiplier=1).then_inc(const_ready, 1)

            def mask(buf, made, ready, heads):
                pool.wait_ge(x_squared, 2 * (QB + 1))
                pool.wait_ge(made, heads)
                for at_z, n in ((0, P), (B1, P), (B3, P), (B2, P), (BTT, TAIL), (BNN, TS)):
                    x = buf[0:n, at_z:at_z + n]
                    last = G.affine_select(out=x, in_=x, compare_op=ALU.is_gt, fill=0.0, base=0,
                                           pattern=[[1, n]], channel_multiplier=-1)
                last.then_inc(ready, 1)

            with pool.Fori(1, HEADS + 1) as heads:
                mask(relu, sp_made, sp_ready, heads)
                mask(soft, w_made, w_ready, heads)

            for c in range(TK):
                pool.wait_ge(mix_hi, c + 1)
                G.tensor_tensor(act_lo[:, c, LATE], wide_c[:, c, LATE], act_hi[:, c, LATE].bitcast(F32),
                                ALU.subtract).then_inc(mix_split[0], 1)

            for c in range(KC):
                pool.wait_ge(sq_made, c + 1)
                add_square(pool, 1, c)

            pool.wait_ge(h_loaded, 16)
            for c in range(KC):
                pool.wait_ge(scaled, c + 1)
                G.tensor_tensor(resid[:, c, LATE], resid[:, c, LATE], wide_c[:, c, LATE], ALU.add).then_inc(h2_ready, 1)
                if c:
                    pool.wait_ge(sq_made, KC + c)
                    add_square(pool, 2, c - 1)
            pool.wait_ge(sq_made, 2 * KC)
            add_square(pool, 2, KC - 1)

            for c in range(KC):
                pool.wait_ge(sq_made, 2 * KC + c + 1)
                add_square(pool, 3, c)
            for c in range(KC):
                pool.wait_ge(y_scaled, c + 1)
                G.tensor_tensor(resid[:, c, LATE], resid[:, c, LATE], wide_c[:, c, LATE], ALU.add).then_inc(y_ready, 1)


_INS = ["x_prompt", "x_sample", "cache_k", "cache_v", "state_conv", "meta", "w_in", "w_out", "conv_w",
        "g_pre_mix", "g_post_mix", "g_attn_out", "g_conv_out", "g_pre_ffn", "g_post_ffn",
        "w_gate", "w_up", "w_down"]


def kernel(**inputs):
    import numpy as _np
    import concourse.bacc as _bacc
    from concourse import mybir as _mybir
    from concourse.bass_utils import run_bass_kernel_spmd as _run

    arrays = {f"in_{n}_dram": _np.ascontiguousarray(inputs[n]) for n in _INS}
    nc = _bacc.Bacc("TRN2", target_bir_lowering=False, num_devices=1)
    args = [nc.dram_tensor(n, a.shape, _mybir.dt.from_np(a.dtype), kind="ExternalInput").ap()
            for n, a in arrays.items()]
    _, seq, d = inputs["x_prompt"].shape
    _, ts, _ = inputs["x_sample"].shape
    tp = inputs["meta"].shape[0] + seq
    depth, _, _, heads, hd = inputs["cache_k"].shape
    state = inputs["state_conv"].shape
    outs = [(1, seq, d), (1, ts, d), (depth, 1, tp, heads, hd), (depth, 1, tp, heads, hd), state,
            (depth, 1, ts, heads, hd), (depth, 1, ts, heads, hd), state]
    for i, shape in enumerate(outs):
        args.append(nc.dram_tensor(f"out_{i}_dram", shape, _mybir.dt.float32, kind="ExternalOutput").ap())
    args.append(nc.dram_tensor("h_scratch", (128, d // 128, tp + ts), _mybir.dt.float32, kind="Internal").ap())
    build_layer(nc, *args)
    r = _run(nc, [arrays], core_ids=[0])
    return tuple(r.results[0][f"out_{i}_dram"] for i in range(len(outs)))
```

```python
from contextlib import ExitStack

import concourse.bass as bass
from concourse import mybir

F32 = mybir.dt.float32
F32R = mybir.dt.float32r
ALU = mybir.AluOpType
ACT = mybir.ActivationFunctionType

P = 128
EPS = 1e-6


def build_layer(nc, x_prompt, x_sample, cache_k, cache_v, state_conv, meta, w_in, w_out, conv_w,
                g_pre_mix, g_post_mix, g_attn_out, g_conv_out, g_pre_ffn, g_post_ffn,
                w_gate, w_up, w_down,
                y_prompt, y_sample, new_k_prompt, new_v_prompt, new_conv_prompt,
                new_k_sample, new_v_sample, new_conv_sample, h_scratch):
    D = x_prompt.shape[2]
    SEQ = x_prompt.shape[1]
    NMETA = meta.shape[0]
    TP = NMETA + SEQ
    TS = x_sample.shape[1]
    T = TP + TS
    HALF = T // 2
    LATE = slice(NMETA, T)
    LHALF = (T - NMETA) // 2
    KC = D // P
    HEADS = cache_k.shape[3]
    GROUPS = conv_w.shape[2] // P
    PAST = cache_k.shape[2]
    DFF = w_gate.shape[2]
    TAIL = TP % P
    MAIN = TP - TAIL
    QB = MAIN // P
    SCALE = float(P) ** -0.5
    assert ((T - NMETA) % 4, QB, TAIL, TS, PAST, HEADS, GROUPS) == (0, 4, 16, 32, 2 * P, 8, 8)

    TK = 8
    LEAD = 3
    SLOTS = 4
    PAIR_T = 12
    IN_T = PAIR_T * (HEADS + GROUPS) // 2
    OUT_T = 2 * KC
    FB = 4
    NFB = DFF // P // FB
    FF_T = FB * 4 + KC // 2
    FF_CH = 2 * FB + KC
    CH_OUT = IN_T // 2
    CH_FF = CH_OUT + KC
    T_OUT = IN_T
    T_FF = IN_T + OUT_T

    BANK = 512
    queries_of = [TP - max(NMETA, j * P) for j in range(QB)]
    B1, B2 = BANK, 2 * BANK
    B3 = B2 + queries_of[2]
    ZW = B3 + queries_of[3]
    BC = B1 + queries_of[1]
    BNN = BC + 2 * TS
    BTT = BNN + TS
    key_block_at = [0, B1, B2, B3]
    assert queries_of[0] == SEQ == BANK and BTT + TAIL == B2

    x_parts = [0, KC // 4, KC // 2, KC]

    C_STATE, C_CONVW = 0, 16
    C_PREMIX, C_POSTMIX = 40, 56
    C_ATTN, C_CONV = 72, 80
    C_PREFFN, C_POSTFFN = 88, 104
    NCOL = 120

    with ExitStack() as ctx:
        def sb(name, shape, dt=F32):
            return ctx.enter_context(nc.sbuf_tensor(name, shape, dt))

        def sem(name):
            return ctx.enter_context(nc.semaphore(name))

        act_hi = sb("act_hi", [P, KC, T], F32R)
        act_lo = sb("act_lo", [P, KC, T], F32R)
        wide = sb("wide", [P, KC * T])
        wide_c = wide[:, :].rearrange("p (c t) -> p c t", c=KC)
        misc = sb("misc", [P, KC * T])
        resid = misc[:, :].rearrange("p (c t) -> p c t", c=KC)
        RAW = 2 * TK * P
        w_raw = sb("w_raw", [P, RAW + T - NMETA])
        w_hi = sb("w_hi", [P, SLOTS, TK * P], F32R)
        w_lo = sb("w_lo", [P, SLOTS, TK * P], F32R)
        rstd = sb("rstd", [P, T])
        buf_g = sb("buf_g", [P, T])
        buf_e = sb("buf_e", [P, T])
        ff_hi = sb("ff_hi", [P, FB, T], F32R)
        ff_lo = sb("ff_lo", [P, FB, T], F32R)
        ident = sb("ident", [P, P])
        neg1_r = sb("neg1", [P, P], F32R)
        neg1 = neg1_r[:, :].bitcast(F32)
        cols = sb("cols", [P, NCOL])
        eps = sb("eps", [P, 1])
        sq_sums = sb("sq_sums", [P, 2, QB + 1])

        def carve(at, n):
            return misc[:, at:at + n], at + n

        at = 0
        qT, at = carve(at, 564)
        kT, at = carve(at, 564)
        vT, at = carve(at, 564)
        vtok_f, at = carve(at, 2 * 6 * P)
        ktok_f, at = carve(at, 6 * P)
        soft, at = carve(at, ZW)
        relu, at = carve(at, ZW)
        kc_tok_f, at = carve(at, 2 * P)
        kcT, at = carve(at, 2 * P)
        vc_f, at = carve(at, 2 * P)
        uext, at = carve(at, TP + TS + 4)
        ulast_f, at = carve(at, 4 * GROUPS)
        assert at <= KC * T
        vtok = vtok_f.rearrange("p (b j d) -> p b j d", b=2, j=6)
        ktok = ktok_f.rearrange("p (j d) -> p j d", j=6)
        kc_tok = kc_tok_f.rearrange("p (j d) -> p j d", j=2)
        vc = vc_f.rearrange("p (j d) -> p j d", j=2)
        ulast = ulast_f.rearrange("p (a g) -> p a g", a=4)
        sp_hi, sp_lo = (ff[:, :, :].rearrange("p f t -> p (f t)")[:, 0:ZW] for ff in (ff_hi, ff_lo))
        tri_r = ff_hi[:, :, :].rearrange("p f t -> p (f t)")[:, ZW:ZW + P]
        tri = tri_r.bitcast(F32)
        sq_hi = ff_hi[:, :, :].rearrange("p f t -> p (f t)")[:, ZW + P:ZW + P + SEQ]
        sq_lo = ff_lo[:, :, :].rearrange("p f t -> p (f t)")[:, ZW:ZW + SEQ]
        x_tok = [wide[:, j * D:(j + 1) * D] for j in range(QB)] + [misc[:, 0:D]]
        RING = 8
        end = D + RING * T
        h_ring = misc[:, D:end].rearrange("p (s t) -> p s t", s=RING)
        col_rows = wide[0:NCOL, QB * D:QB * D + P]
        squares_out = misc[:, end:end + D].rearrange("p (s n) -> p s n", s=2)
        assert end + D <= KC * T
        squares = [buf_e[:, LATE], w_raw[:, RAW:RAW + T - NMETA]]
        y_tok = w_raw[:, 0:4 * (QB + 1) * P].rearrange("p (s j f) -> p s j f", s=4, j=5)

        ps = ctx.enter_context(nc.psum_tensor("ps", [P, 8, 512], F32))
        acc = [ps[:, 2 * s:2 * s + 2, 0:HALF] for s in range(2)]
        acc_late = [ps[:, 2 * s:2 * s + 2, 0:LHALF] for s in range(2)]

        def x_bank(c, j):
            n = P if j < QB else TAIL + TS
            return ps[:, 2 + 2 * (c % 3) + j // 3, (j % 3) * P:(j % 3) * P + n]

        bank_a, bank_b, bank_c, bank_d = (ps[:, 4 + j, :] for j in range(4))
        score_banks = [bank_a, bank_b, bank_c]

        x_loaded = [[sem(f"x_loaded{j}_{h}") for h in range(3)] for j in range(QB + 1)]
        cols_loaded = sem("cols_loaded")
        const_ready = sem("const_ready")
        pool_step = sem("pool_step")
        cols_turned = sem("cols_turned")
        cols_ready = sem("cols_ready")
        x_turned = sem("x_turned")
        h_left = sem("h_left")
        h_right = sem("h_right")
        x_hi_ready = sem("x_hi_ready")
        x_ready = sem("x_ready")
        x_squared = sem("x_squared")
        x_summed = sem("x_summed")
        diag_ready = sem("diag_ready")
        h_stored = [sem(f"h_stored{j}") for j in range(RING)]
        sq_made = sem("sq_made")
        sq_added = sem("sq_added")
        ms_ready = sem("ms_ready")
        ms_log = sem("ms_log")
        rstd_ready = sem("rstd_ready")
        w_loaded = [sem(f"w_loaded{j}") for j in range(2)]
        hi_ready = sem("hi_ready")
        lo_ready = sem("lo_ready")
        first_used = sem("first_used")
        chunk_done = sem("chunk_done")
        chunk_copied = sem("chunk_copied")
        kc_loaded = sem("kc_loaded")
        vc_loaded = sem("vc_loaded")
        kc_turned = sem("kc_turned")
        kc_copied = sem("kc_copied")
        v_turned = sem("v_turned")
        v_copied = sem("v_copied")
        k_turned = sem("k_turned")
        k_copied = sem("k_copied")
        ends_turned = sem("ends_turned")
        ends_copied = sem("ends_copied")
        k_stored = sem("k_stored")
        v_stored = [sem(f"v_stored{j}") for j in range(2)]
        z_ready = sem("z_ready")
        abs_ready = sem("abs_ready")
        exp_ready = sem("exp_ready")
        log_ready = sem("log_ready")
        sp_made = sem("sp_made")
        sp_ready = sem("sp_ready")
        sp_hi_ready = sem("sp_hi_ready")
        sp_split = sem("sp_split")
        e_ready = sem("e_ready")
        w_made = sem("w_made")
        w_ready = sem("w_ready")
        o_ready = sem("o_ready")
        o_copied = sem("o_copied")
        sq_ready = sem("sq_ready")
        sq_hi_ready = sem("sq_hi_ready")
        sq_split = sem("sq_split")
        n1_ready = sem("n1_ready")
        n1_log = sem("n1_log")
        n2_ready = sem("n2_ready")
        n2_log = sem("n2_log")
        norm_ready = sem("norm_ready")
        mixed = sem("mixed")
        bank_b_clear = sem("bank_b_clear")
        c_scaled = sem("c_scaled")
        u_ends = sem("u_ends")
        conv_step = sem("conv_step")
        ulast_turned = sem("ulast_turned")
        ulast_copied = sem("ulast_copied")
        conv_stored = sem("conv_stored")
        mix_hi = sem("mix_hi")
        mix_split = [sem("mix_split0"), sem("mix_split1")]
        h_loaded = sem("h_loaded")
        scaled = sem("scaled")
        h2_ready = [sem("h2_dve"), sem("h2_pool")]
        f_hi = sem("f_hi")
        f_split = sem("f_split")
        e_neg = sem("e_neg")
        gate_scaled = sem("gate_scaled")
        ff_step = sem("ff_step")
        ff_hi_ready = sem("ff_hi_ready")
        ff_ready = sem("ff_ready")
        y_scaled = sem("y_scaled")
        y_ready = [sem("y_dve"), sem("y_pool")]
        y_turned = sem("y_turned")
        y_copied = sem("y_copied")
        y_stored = [sem(f"y_stored{j}") for j in range(4)]

        def tile_no(phase, k):
            per, r, first = phase
            return r * per + first + k

        def known(x):
            return isinstance(x, int)

        def loads_of(phase, k):
            per, r, first = phase
            return r * (per // 2) + (first + k) // 2 + 1

        def tile_used(phase, k):
            per, r, first = phase
            if per == FF_T:
                if k < 0:
                    return chunk_done, r * FF_CH + CH_FF + 2 * (k + 1)
                if k >= 4 * FB:
                    return chunk_done, r * FF_CH + CH_FF + 2 * FB + 2 * (k - 4 * FB + 1)
                if k % 2:
                    return chunk_done, r * FF_CH + CH_FF + k // 2 + 1
                return first_used, r * 2 * FB + CH_FF + k // 2 + 1
            sem_of = (first_used, chunk_done)[k % 2]
            return sem_of, r * (per // 2) + (first + k) // 2 + 1

        def h2_adder(c):
            return int(c % 3 == 2)

        def y_adder(c):
            return int(c % 3 != 2)

        def added(adder, done, c):
            return done[adder(c)], sum(adder(x) == adder(c) for x in range(c + 1))

        def h2_made(c):
            return added(h2_adder, h2_ready, c)

        def y_made(c):
            return added(y_adder, y_ready, c)

        block = ctx.enter_context(nc.Block())

        def raw_slot(k):
            return w_raw[:, (k % 2) * TK * P:(k % 2 + 1) * TK * P]

        def round_weights(phase, k):
            t = tile_no(phase, k)
            nc.scalar.wait_ge(w_loaded[k % 2], 16 * loads_of(phase, k))
            if not known(t) or t >= SLOTS:
                nc.scalar.wait_ge(*tile_used(phase, k - SLOTS))
            nc.scalar.copy(w_hi[:, k % SLOTS, :], raw_slot(k)).then_inc(hi_ready, 1)

        def rest_of_weights(phase, k, engine=nc.vector):
            t = tile_no(phase, k)
            engine.wait_ge(hi_ready, t + 1)
            engine.tensor_tensor(w_lo[:, k % SLOTS, :], raw_slot(k),
                                 w_hi[:, k % SLOTS, :].bitcast(F32), ALU.subtract).then_inc(lo_ready, 1)

        def multiply(slot, nk, width, col, x_hi, x_lo, x_at, out, ks, first, last):
            half = out.shape[2]
            token = T - 2 * half
            hi = w_hi[:, slot, :].rearrange("p (k n) -> p k n", k=nk)
            lo = w_lo[:, slot, :].rearrange("p (k n) -> p k n", k=nk)
            for k in ks:
                for w, x, begins, ends in ((hi, x_hi, first and k == 0, False), (hi, x_lo, False, False),
                                           (lo, x_hi, False, last and k == nk - 1)):
                    for h in range(2):
                        mm = nc.tensor.matmul(out[:, h, :], w[:, k, col:col + width],
                                              x[:, x_at + k, token + h * half:token + (h + 1) * half],
                                              start=begins, stop=ends)
            return mm

        w_in_v = w_in[0].rearrange("(k p) n -> p k n", p=P)
        w_out_v = w_out[0].rearrange("(k p) n -> p k n", p=P)
        w_gate_v = w_gate[0].rearrange("(k p) n -> p k n", p=P)
        w_up_v = w_up[0].rearrange("(k p) n -> p k n", p=P)
        w_down_v = w_down[0].rearrange("(b k p) n -> p b k n", k=FB, p=P)
        AW = HEADS * P
        h_scr = h_scratch

        @block.sync
        def _(sp):
            xp = x_prompt[0]

            def load_x(h):
                f = slice(x_parts[h] * P, x_parts[h + 1] * P)
                sp.dma_start(x_tok[0][0:NMETA, f], meta[:, f]).then_inc(x_loaded[0][h], 16)
                sp.dma_start(x_tok[0][NMETA:P, f], xp[0:P - NMETA, f]).then_inc(x_loaded[0][h], 16)
                for j in range(1, QB):
                    sp.dma_start(x_tok[j][:, f], xp[j * P - NMETA:(j + 1) * P - NMETA, f])\
                      .then_inc(x_loaded[j][h], 16)
                sp.dma_start(x_tok[QB][0:TAIL, f], xp[SEQ - TAIL:SEQ, f]).then_inc(x_loaded[QB][h], 16)
                sp.dma_start(x_tok[QB][TAIL:TAIL + TS, f], x_sample[0][:, f]).then_inc(x_loaded[QB][h], 16)

            def load(phase, k, src):
                t = tile_no(phase, k)
                if not known(t) or t >= 2:
                    sp.wait_ge(lo_ready, t - 1)
                dst = raw_slot(k).rearrange("p (k n) -> p k n", k=src.shape[-2])
                sp.dma_start(dst, src).then_inc(w_loaded[k % 2], 16)

            def load_pair(p, bases):
                phase = (PAIR_T, p, 0)
                q = 2 * (p if bases[0] < 3 * AW else p - HEADS // 2)
                for k in range(PAIR_T):
                    u, c, half = k // 6, k % 6 // 2, k % 2
                    load(phase, k, w_in_v[:, TK * half:TK * (half + 1), :]
                         .rearrange("p k (h n) -> p k h n", n=P)[:, :, bass.ds(q + bases[c] // P + u, 1), :]
                         .rearrange("p k h n -> p k (h n)"))

            HEAD_COLS = (2 * AW, AW, 0)
            CONV_COLS = (3 * AW, 3 * AW + GROUPS * P, 3 * AW + 2 * GROUPS * P)
            phase0 = (PAIR_T, 0, 0)
            def load_first(k):
                u, c, half = k // 6, k % 6 // 2, k % 2
                load(phase0, k, w_in_v[:, TK * half:TK * (half + 1),
                                       HEAD_COLS[c] + u * P:HEAD_COLS[c] + (u + 1) * P])
            load_x(0)
            load_first(0)
            load_x(1)
            load_x(2)
            load_first(1)
            for j in range(QB + 1):
                sp.wait_ge(x_loaded[j][2], 32 if j in (0, QB) else 16)
            for c in range(KC):
                if c in (8, 12):
                    load_first(c // 4)
                sp.wait_ge(h_left, c + 1)
                sp.wait_ge(h_right, c + 1)
                sp.dma_start(h_scr[:, c, :], h_ring[:, c % RING, :]).then_inc(h_stored[c % RING], 16)
            for k in range(4, PAIR_T):
                load_first(k)
            with sp.Fori(0, HEADS // 2 - 1) as r:
                load_pair(r + 1, HEAD_COLS)
            with sp.Fori(HEADS // 2, (HEADS + GROUPS) // 2) as p:
                load_pair(p, CONV_COLS)

            def load_out(q):
                at_col = q * 2 * P
                for k in range(4):
                    load((4, q, T_OUT), k, w_out_v[:, TK * (k % 2):TK * (k % 2 + 1),
                                                   bass.ds(at_col + k // 2 * P, P)])
            for q in range(2):
                load_out(q)
            sp.wait_ge(mixed, HEADS + GROUPS)
            sp.wait_ge(conv_stored, 32)
            sp.wait_ge(k_stored, 48 * HEADS)
            for j in range(2):
                sp.wait_ge(v_stored[j], 48 * HEADS // 2)
            for j in range(RING):
                sp.wait_ge(h_stored[j], 16 * (KC // RING))
            sp.dma_start(resid, h_scr).then_inc(h_loaded, 16)
            with sp.Fori(2, KC // 2) as q:
                load_out(q)

            with sp.Fori(0, NFB) as b:
                phase = (FF_T, b, T_FF)
                for k in range(4 * FB):
                    f, src = k // 4, (w_gate_v, w_up_v)[k % 4 // 2]
                    load(phase, k, src[:, TK * (k % 2):TK * (k % 2 + 1), bass.ds(b * FB * P + f * P, P)])
                for m in range(KC // 2):
                    load(phase, 4 * FB + m, w_down_v[:, bass.ds(b, 1), :, 2 * P * m:2 * P * (m + 1)]
                         .rearrange("p b k n -> p (b k) n"))

            for c in range(KC):
                s, f = c % 4, slice(c * P, (c + 1) * P)
                sp.wait_ge(y_copied, c + 1)
                sp.dma_start(y_prompt[0][:, f].rearrange("(j p) n -> p j n", p=P), y_tok[:, s, 0:QB, :])\
                  .then_inc(y_stored[s], 16)
                sp.dma_start(y_sample[0][:, f], y_tok[0:TS, s, QB, :]).then_inc(y_stored[s], 16)
            for s in range(4):
                sp.wait_ge(y_stored[s], 32 * (KC // 4))

        @block.tensor
        def _(pe):
            acts = (act_hi, act_lo)
            hidden = (ff_hi, ff_lo)
            halves_of_tile = (list(range(TK // 2)), list(range(TK // 2, TK)))

            def chunk(phase, k, no, points, late=False):
                if not known(no) or no >= 2:
                    pe.wait_ge(chunk_copied, no - 1)
                out = (acc_late if late or phase[0] != PAIR_T else acc)[(k // 2) % 2]
                for half in range(2):
                    pe.wait_ge(lo_ready, tile_no(phase, k + half) + 1)
                    for part in range(2):
                        mm = multiply((k + half) % SLOTS, TK, P, 0, *acts, TK * half, out,
                                      halves_of_tile[part], half == 0, half == 1)
                        if part == 0:
                            points[2 * half]()
                    mm.then_inc((first_used, chunk_done)[half], 1)
                    points[2 * half + 1]()

            def turn(out, src, n):
                return nc.tensor.transpose(out, src, ident[0:n, 0:n])

            pe.wait_ge(const_ready, 4)
            for c in range(KC + 3):
                if c < KC:
                    if c >= 3:
                        pe.wait_ge(h_left, c - 2)
                        pe.wait_ge(h_right, c - 2)
                    if c == 2:
                        pe.wait_ge(cols_ready, 1)
                    for j in range(QB + 1):
                        if c in x_parts:
                            pe.wait_ge(x_loaded[j][x_parts.index(c)], 32 if j in (0, QB) else 16)
                        n = P if j < QB else TAIL + TS
                        mm = turn(x_bank(c, j), x_tok[j][0:n, c * P:(c + 1) * P], n)
                    mm.then_inc(x_turned, 1)
                if c == 1:
                    pe.wait_ge(cols_loaded, 16 * 8)
                    turn(bank_d[:, 0:NCOL], col_rows, NCOL).then_inc(cols_turned, 1)
                if c >= 3:
                    k = c - 3
                    if k % TK == 0:
                        pe.wait_ge(lo_ready, k // TK + 1)
                    pe.wait_ge(x_ready, k + 1)
                    mm = multiply(k // TK, TK, P, 0, act_hi, act_lo, k // TK * TK, acc[0], [k % TK],
                                  k < TK, k >= TK)
                    if k % TK == TK - 1:
                        mm.then_inc((first_used, chunk_done)[k // TK], 1)
            pe.wait_ge(h_left, KC)
            pe.wait_ge(h_right, KC)

            def input_sums():
                pe.wait_ge(diag_ready, 1)
                for j in range(QB + 1):
                    n = P if j < QB else TAIL + TS
                    mm = nc.tensor.matmul((bank_a, bank_b)[j // 4][:, j % 4 * P:j % 4 * P + n], neg1[0:n, :],
                                          buf_e[0:n, j * P:j * P + n], start=j % 4 == 0, stop=True,
                                          skip_group_check=True)
                mm.then_inc(ms_ready, 1)

            def row_sums(r):
                pe.wait_ge(sq_added, (KC - 1) * r)
                for part, x in enumerate((buf_g[:, LATE], squares[(KC - 1) % 2])):
                    if part:
                        pe.wait_ge(sq_made, KC * r)
                    for h, bank in enumerate((bank_a, bank_b)):
                        mm = nc.tensor.matmul(bank[:, 0:LHALF], neg1[:, :], x[:, h * LHALF:(h + 1) * LHALF],
                                              start=part == 0, stop=part == 1)
                mm.then_inc(ms_ready, 1)

            def into(out, w, x, start=False):
                return nc.tensor.matmul(out, w, x, start=start, stop=True, skip_group_check=True)

            def scores(a):
                pe.wait_ge(chunk_copied, 3 * a + 3)
                pe.wait_ge(kc_copied, a + 1)
                if known(a) and a == 0:
                    pe.wait_ge(bank_b_clear, 1)
                else:
                    pe.wait_ge(o_copied, a)
                into(bank_a, kT[:, 0:P], qT[:, NMETA:TP], start=True)
                into(bank_b[:, 0:queries_of[1]], kT[:, P:2 * P], qT[:, P:TP], start=True)
                into(bank_c[:, 0:B3 - B2], kT[:, 2 * P:3 * P], qT[:, 2 * P:TP], start=True)
                into(bank_c[:, B3 - B2:ZW - B2], kT[:, 3 * P:4 * P], qT[:, 3 * P:TP])
                for j in range(2):
                    at_b = BC - B1 + j * TS
                    into(bank_b[:, at_b:at_b + TS], kcT[:, j * P:(j + 1) * P], qT[:, TP:T])
                into(bank_b[0:TAIL, BTT - B1:BANK], kT[:, MAIN:TP], qT[:, MAIN:TP])
                into(bank_b[0:TS, BNN - B1:BTT - B1], kT[:, TP:T], qT[:, TP:T]).then_inc(z_ready, 1)

            def exponents(a):
                pe.wait_ge(sp_split, a + 1)
                def wide_sum(out, w, at_z, n):
                    into(out, w, sp_hi[:, at_z:at_z + n])
                    into(out, w, sp_lo[:, at_z:at_z + n])
                wide_sum(bank_a, tri_r, 0, BANK)
                wide_sum(bank_b[:, 0:BNN - B1], tri_r, B1, BNN - B1)
                wide_sum(bank_c[:, 0:ZW - B2], tri_r, B2, ZW - B2)
                into(bank_b[0:TAIL, BTT - B1:BANK], tri[0:TAIL, 0:TAIL], relu[0:TAIL, BTT:B2])
                into(bank_b[0:TS, BNN - B1:BTT - B1], tri[0:TS, 0:TS], relu[0:TS, BNN:BTT])

                def last_queries(i, n):
                    end = key_block_at[i] % BANK + queries_of[i]
                    return score_banks[key_block_at[i] // BANK][:, end - n:end]

                for j in range(1, QB):
                    n = queries_of[j]
                    for i in range(j):
                        if n >= 256:
                            wide_sum(last_queries(i, n), neg1_r[:, :], key_block_at[j], n)
                        else:
                            into(last_queries(i, n), neg1, relu[:, key_block_at[j]:key_block_at[j] + n])
                for i in range(QB):
                    into(last_queries(i, TAIL), neg1[0:TAIL, :], relu[0:TAIL, BTT:B2])
                into(bank_b[:, BC - B1:BC - B1 + TS], neg1, relu[:, BC + TS:BC + 2 * TS])
                new = relu[0:TS, BNN:BTT]
                into(bank_b[:, BC - B1:BNN - B1].rearrange("p (b n) -> p b n", b=2), neg1[0:TS, :],
                     new.unsqueeze(1).broadcast_to([TS, 2, TS])).then_inc(e_ready, 1)

            def attend(a, par, bank_free):
                pe.wait_ge(w_ready, a + 1)
                pe.wait_ge(ends_copied, a + 1)
                pe.wait_ge(vc_loaded, 16 * (a + 1))
                pe.wait_ge(*bank_free)
                v = vtok[:, par]
                for j in range(QB):
                    n = queries_of[j]
                    into(bank_d[:, BANK - n:BANK], v[:, j, :], soft[:, key_block_at[j]:key_block_at[j] + n],
                         start=j == 0)
                into(bank_d[:, BANK - TAIL:BANK], v[0:TAIL, QB, :], soft[0:TAIL, BTT:B2])
                for j in range(2):
                    into(bank_c[:, 0:TS], vc[:, j, :], soft[:, BC + j * TS:BC + (j + 1) * TS], start=j == 0)
                into(bank_c[:, 0:TS], v[0:TS, QB + 1, :], soft[0:TS, BNN:BTT]).then_inc(o_ready, 1)

            def norm_main(n, *bank_free):
                pe.wait_ge(sq_split, n + 1)
                pe.wait_ge(*bank_free)
                into(bank_d, neg1_r[:, :], sq_hi, start=True)
                into(bank_d, neg1_r[:, :], sq_lo).then_inc(n1_ready, 1)

            def norm_ends(n, bank=None):
                if bank is None:
                    pe.wait_ge(n1_log, n + 1)
                    bank = bank_d
                into(bank[:, 256:256 + TS], neg1, buf_e[:, TP:T], start=True)\
                    .then_inc(n2_ready, 1)

            def turn_cache(i, *bank_free):
                pe.wait_ge(kc_loaded, 16 * (i + 1))
                pe.wait_ge(*bank_free)
                for j in range(2):
                    mm = turn(bank_d[:, j * P:(j + 1) * P], kc_tok[:, j, :], P)
                mm.then_inc(kc_turned, 1)

            def turn_main(src, done, copied, bank_free):
                pe.wait_ge(*copied)
                pe.wait_ge(*bank_free)
                for j in range(QB):
                    mm = turn(bank_d[:, j * P:(j + 1) * P], src[:, j * P:(j + 1) * P], P)
                mm.then_inc(done, 1)

            def turn_ends(i):
                pe.wait_ge(k_copied, i + 1)
                for j, src in enumerate((vT, kT)):
                    turn(bank_d[0:TAIL, j * P:(j + 1) * P], src[:, MAIN:TP], P)
                    mm = turn(bank_d[0:TS, (2 + j) * P:(3 + j) * P], src[:, TP:T], P)
                mm.then_inc(ends_turned, 1)

            def walk(p, u, i, at_point, late, begin=0):
                for c in range(begin, 3):
                    points = [at_point.get(4 * c + m, lambda: None) for m in range(1, 5)]
                    chunk((PAIR_T, p, 0), 6 * u + 2 * c, 3 * i + c, points, c == late)

            def head(p, u, i, has_attention, has_norm):
                a, n = i - 1, i - 2

                def after_first_tile():
                    if has_attention:
                        scores(a)
                    if has_norm:
                        norm_main(n, ends_copied, i)

                def after_half_of_k():
                    if not has_attention:
                        input_sums()
                    turn_cache(i, *((n2_log, n + 1) if has_norm else (ends_copied, i) if has_attention
                                    else (cols_ready, 1)))

                at_point = {
                    2: after_first_tile,
                    5: after_half_of_k,
                    6: lambda: turn_main(vT, v_turned, (chunk_copied, 3 * i + 1), (kc_copied, i + 1)),
                    11: lambda: turn_main(kT, k_turned, (chunk_copied, 3 * i + 2),
                                          (o_copied, i) if has_attention else (v_copied, i + 1)),
                }
                if has_norm:
                    at_point[4] = lambda: norm_ends(n)
                if has_attention:
                    at_point[1] = lambda: turn_ends(a)
                    at_point[7] = lambda: exponents(a)
                    at_point[9] = lambda: attend(a, (u + 1) % 2, (v_copied, i + 1))
                if not known(i) or i > 0:
                    walk(p, u, i, at_point, 2)
                else:
                    walk(p, u, i, at_point, 2, begin=1)

            def group(p, u, i, first_pair=False):
                last = HEADS - 1
                if first_pair and u == 0:
                    def after_first_tile():
                        scores(last)
                        norm_main(last - 1, ends_copied, HEADS)
                    at_point = {1: lambda: turn_ends(last), 2: after_first_tile,
                                4: lambda: norm_ends(last - 1), 7: lambda: exponents(last),
                                9: lambda: attend(last, last % 2, (n2_log, last))}
                else:
                    at_point = {6: lambda: norm_main(i - 1, n2_log, i - 1), 8: lambda: norm_ends(i - 1)}
                    if first_pair:
                        at_point[2] = lambda: norm_main(last, o_copied, HEADS)
                        at_point[4] = lambda: norm_ends(last)
                walk(p, u, i, at_point, 0)

            for u in range(2):
                head(0, u, u, u > 0, False)
            with pe.Fori(1, HEADS // 2) as p:
                for u in range(2):
                    head(p, u, 2 * p + u, True, True)
            for u in range(2):
                group(HEADS // 2, u, HEADS + u, first_pair=True)
            with pe.Fori(HEADS // 2 + 1, (HEADS + GROUPS) // 2) as p:
                for u in range(2):
                    group(p, u, 2 * p + u)

            no_points = [lambda: None] * 4

            def last_norm_and_rows():
                norm_main(HEADS + GROUPS - 1, n2_log, HEADS + GROUPS - 1)
                norm_ends(HEADS + GROUPS - 1, bank_c)
                pe.wait_ge(u_ends, GROUPS)
                turn(bank_a[0:4 * GROUPS, 0:P], ulast_f, P).then_inc(ulast_turned, 1)

            def mix_chunk(c):
                return mix_split[c // TK], c % TK + 1

            def two_chunks(tile0, x_wait, lag, between):
                for c in range(KC + lag):
                    for j, k in ((0, c), (1, c - lag)):
                        if not 0 <= k < KC:
                            continue
                        if k % TK == 0:
                            pe.wait_ge(lo_ready, tile0 + 2 * j + k // TK + 1)
                        if j == 0:
                            pe.wait_ge(*x_wait(c))
                        mm = multiply(2 * j + k // TK, TK, P, 0, act_hi, act_lo, k // TK * TK, acc_late[j],
                                      [k % TK], k < TK, k >= TK)
                        if k % TK == TK - 1:
                            mm.then_inc((first_used, chunk_done)[k // TK], 1)
                    if c in between:
                        between[c]()

            pe.wait_ge(chunk_copied, CH_OUT)
            two_chunks(T_OUT, mix_chunk, 2, {6: last_norm_and_rows})
            with pe.Fori(1, KC // 2) as q:
                for c in range(2):
                    chunk((4, q, T_OUT), 2 * c, 2 * q + CH_OUT + c, no_points)
            row_sums(1)

            def ffn_block(b, first):
                phase = (FF_T, b, T_FF)
                ch = b * FF_CH + CH_FF
                if first:
                    pe.wait_ge(chunk_copied, CH_FF)
                    two_chunks(T_FF, lambda c: (f_split, c + 1), 1, {})
                    row_sums(2)
                for j in range(2 if first else 0, 2 * FB):
                    chunk(phase, 2 * j, ch + j, no_points)
                for m in range(KC // 2):
                    k = 4 * FB + m
                    pe.wait_ge(lo_ready, tile_no(phase, k) + 1)
                    for ks in ((range(FB - 1), range(FB - 1, FB)) if m == 0 else (range(FB),)):
                        for o in range(2):
                            no = ch + 2 * FB + 2 * m + o
                            if ks[0] == 0:
                                pe.wait_ge(chunk_copied, no - 1)
                            for kk in ks:
                                if m == 0 and o == 0:
                                    pe.wait_ge(ff_ready, b * FB + kk + 1)
                                mm = multiply(k % SLOTS, FB, P, o * P, *hidden, 0, acc_late[o], [kk],
                                              True, True)
                            if ks[-1] == FB - 1:
                                mm.then_inc(chunk_done, 1)

            ffn_block(0, True)
            with pe.Fori(1, NFB) as b:
                ffn_block(b, False)

            row_sums(3)
            for c in range(KC):
                s = c % 4
                pe.wait_ge(*y_made(c))
                if c >= 4:
                    pe.wait_ge(y_copied, c - 3)
                for j in range(QB + 1):
                    n = P if j < QB else TS
                    at_t = NMETA + j * P
                    mm = turn(ps[0:n, 2 * s + j // 3, (j % 3) * P:(j % 3 + 1) * P],
                              resid[:, c, at_t:at_t + n], P)
                mm.then_inc(y_turned, 1)

        @block.scalar
        def _(act):
            A = nc.scalar.activation
            kp = new_k_prompt[0, 0].rearrange("t h d -> h t d")
            vp = new_v_prompt[0, 0].rearrange("t h d -> h t d")
            ks = new_k_sample[0, 0].rearrange("t h d -> h t d")
            vs = new_v_sample[0, 0].rearrange("t h d -> h t d")
            kc_v = cache_k[0, 0].rearrange("(j p) h d -> p j h d", p=P)
            vc_v = cache_v[0, 0].rearrange("(j p) h d -> p j h d", p=P)

            def load_cache(cache, i, dst, done):
                act.dma_start(dst, cache[:, :, bass.ds(i, 1), :].rearrange("p j h d -> p (j h) d"))\
                   .then_inc(done, 16)

            def store_head(prompt, sample, i, src, done):
                act.dma_start(prompt[bass.ds(i, 1), 0:MAIN, :].rearrange("h (j p) d -> p (h j) d", p=P),
                              src[:, 0:QB, :]).then_inc(done, 16)
                act.dma_start(prompt[bass.ds(i, 1), MAIN:TP, :].rearrange("h p d -> p (h d)"),
                              src[0:TAIL, QB, :]).then_inc(done, 16)
                act.dma_start(sample[bass.ds(i, 1), :, :].rearrange("h p d -> p (h d)"),
                              src[0:TS, QB + 1, :]).then_inc(done, 16)

            def make_rstd(r):
                act.wait_ge(ms_ready, r + 1)
                out = rstd[:, LATE if r else slice(0, T)]
                if r:
                    A(out.rearrange("p (h t) -> p h t", h=2), ps[:, 4:6, 0:LHALF], ACT.Ln,
                      scale=-1.0 / D, bias=eps[:, 0:1]).then_inc(ms_log, 1)
                else:
                    A(out[:, 0:MAIN], bank_a[:, 0:MAIN], ACT.Ln, scale=-1.0 / D, bias=eps[:, 0:1])
                    A(out[:, MAIN:T], bank_b[:, 0:T - MAIN], ACT.Ln, scale=-1.0 / D, bias=eps[:, 0:1])\
                        .then_inc(ms_log, 1)
                act.wait_ge(ms_log, r + 1)
                A(out, out, ACT.Exp, scale=-0.5).then_inc(rstd_ready, 1)

            def load_log_table(r):
                A(sq_sums[:, 1, r:r + 1], eps[:, 0:1], ACT.Ln)

            def norm_log_main(n):
                act.wait_ge(n1_ready, n + 1)
                A(buf_e[:, NMETA:TP], bank_d, ACT.Ln, scale=-1.0 / P, bias=eps[:, 0:1])\
                    .then_inc(n1_log, 1)

            def norm_finish(n, bank=bank_d):
                act.wait_ge(n2_ready, n + 1)
                A(buf_e[:, TP:T], bank[:, 256:256 + TS], ACT.Ln, scale=-1.0 / P, bias=eps[:, 0:1])\
                    .then_inc(n2_log, 1)
                act.wait_ge(n2_log, n + 1)
                A(buf_e[:, LATE], buf_e[:, LATE], ACT.Exp, scale=-0.5).then_inc(norm_ready, 1)

            parts = ((bank_a, 0, 512), (bank_b, 512, 512), (bank_c, B2, ZW - B2))

            def soft_begin(a):
                act.wait_ge(z_ready, a + 1)
                for bank, at_z, n in parts:
                    A(soft[:, at_z:at_z + n], bank[:, 0:n], ACT.Abs)
                for bank, at_z, n in parts:
                    last = A(relu[:, at_z:at_z + n], bank[:, 0:n], ACT.Relu)
                last.then_inc(abs_ready, 1)

            def soft_finish(a):
                act.wait_ge(abs_ready, a + 1)
                A(soft, soft, ACT.Exp, scale=-1.0).then_inc(exp_ready, 1)
                act.wait_ge(exp_ready, a + 1)
                A(soft, soft, ACT.Ln, bias=1.0).then_inc(log_ready, 1)

            def softplus_high(a):
                act.wait_ge(sp_ready, a + 1)
                A(sp_hi, relu, ACT.Copy).then_inc(sp_hi_ready, 1)

            def weights_of(a):
                act.wait_ge(e_ready, a + 1)
                for bank, at_z, n in parts:
                    last = A(soft[:, at_z:at_z + n], bank[:, 0:n], ACT.Exp)
                last.then_inc(w_made, 1)

            def square_mix(src, n, ready):
                act.wait_ge(*ready)
                if not known(n) or n > 0:
                    act.wait_ge(mixed, n)
                A(buf_e[:, LATE], src[:, LATE], ACT.Square).then_inc(sq_ready, 1)
                act.wait_ge(sq_ready, n + 1)
                A(sq_hi, buf_e[:, NMETA:TP], ACT.Copy).then_inc(sq_hi_ready, 1)

            def square_row(src, r, c, par):
                if not known(c) or c > 1:
                    act.wait_ge(sq_added, (KC - 1) * (r - 1) + c - 1)
                out = squares[par]
                if len(src.shape) == 3:
                    out = out.rearrange("p (h t) -> p h t", h=2)
                A(out, src, ACT.Square).then_inc(sq_made, 1)

            for at_col, rows in ((C_STATE, state_conv[0, 0]), (C_CONVW, conv_w[0]),
                                 (C_PREMIX, g_pre_mix), (C_POSTMIX, g_post_mix),
                                 (C_ATTN, g_attn_out), (C_CONV, g_conv_out),
                                 (C_PREFFN, g_pre_ffn), (C_POSTFFN, g_post_ffn)):
                rows = rows.rearrange("a (g p) -> (a g) p", p=P)
                act.dma_start(col_rows[at_col:at_col + rows.shape[0], :], rows).then_inc(cols_loaded, 16)

            def square_x(h, j):
                n = P if j < QB else TAIL + TS
                k = (QB + 1) * h + j
                for part in ((0, 1), (2,))[h]:
                    act.wait_ge(x_loaded[j][part], 32 if j in (0, QB) else 16)
                if k >= 2:
                    act.wait_ge(x_squared, k - 1)
                A(squares_out[0:n, k % 2, :],
                  x_tok[j][0:n, h * D // 2:(h + 1) * D // 2], ACT.Square,
                  accum_out=sq_sums[0:n, h, j:j + 1]).then_inc(x_squared, 1)

            act.wait_ge(const_ready, 4)
            A(rstd[:, 0:1], eps[:, 0:1], ACT.Copy)

            def copy_right(c):
                act.wait_ge(x_turned, c + 1)
                if c >= RING:
                    act.wait_ge(h_stored[c % RING], 16 * (c // RING))
                    act.wait_ge(x_ready, c - RING + 1)
                A(h_ring[:, c % RING, 3 * P:T], ps[:, 3 + 2 * (c % 3), 0:T - 3 * P], ACT.Copy)\
                    .then_inc(h_right, 1)

            copy_right(0)
            round_weights((PAIR_T, 0, 0), 0)
            for c in range(KC):
                s = c % RING
                if c + 1 < KC:
                    copy_right(c + 1)
                if c == 0:
                    act.wait_ge(cols_ready, 1)
                act.wait_ge(h_left, c + 1)
                act.wait_ge(h_right, c + 1)
                A(act_hi[:, c, :], h_ring[:, s, :], ACT.Copy, scale=cols[:, C_PREMIX + c:C_PREMIX + c + 1])\
                    .then_inc(x_hi_ready, 1)
                if c % 2:
                    square_x(c // 2 // (QB + 1), c // 2 % (QB + 1))
                if c in (6, 12):
                    round_weights((PAIR_T, 0, 0), c // 6)
            for j in range(KC // 2 - QB - 1, QB + 1):
                square_x(1, j)

            def head(p, u, i, has_attention, has_norm):
                a, n = i - 1, i - 2
                for s in range(6):
                    if s == 1 and has_attention:
                        soft_finish(a)
                        if has_norm:
                            norm_finish(n)
                    round_weights((PAIR_T, p, 0), 6 * u + s + LEAD)
                    if s == 0:
                        if has_attention:
                            act.wait_ge(kc_turned, i)
                        else:
                            act.wait_ge(x_squared, 2 * (QB + 1))
                            for j in range(RING):
                                act.wait_ge(h_stored[j], 16 * (KC // RING))
                        load_cache(kc_v, i, kc_tok, kc_loaded)
                        if has_norm:
                            norm_log_main(n)
                        if has_attention:
                            soft_begin(a)
                    if s == 1:
                        if not has_attention:
                            make_rstd(0)
                        if has_attention:
                            softplus_high(a)
                            act.wait_ge(ends_copied, a + 1)
                            store_head(kp, ks, a, ktok, k_stored)
                            store_head(vp, vs, a, vtok[:, (u + 1) % 2], v_stored[(u + 1) % 2])
                    if s == 3 and has_attention:
                        weights_of(a)
                    if s == 4:
                        if has_attention:
                            square_mix(buf_g[:, :], a, (o_copied, a + 1))
                            act.wait_ge(o_ready, i)
                        load_cache(vc_v, i, vc, vc_loaded)

            def group(p, u, i, first_pair=False):
                last = HEADS - 1
                for s in range(6):
                    if s == 1 and first_pair and u == 0:
                        soft_finish(last)
                        norm_finish(last - 1)
                    round_weights((PAIR_T, p, 0), 6 * u + s + LEAD)
                    if first_pair and u == 0:
                        if s == 0:
                            norm_log_main(last - 1)
                            soft_begin(last)
                        if s == 1:
                            softplus_high(last)
                            act.wait_ge(ends_copied, HEADS)
                            store_head(kp, ks, last, ktok, k_stored)
                            store_head(vp, vs, last, vtok[:, last % 2], v_stored[last % 2])
                        if s == 3:
                            weights_of(last)
                        if s == 4:
                            square_mix(buf_g[:, :], last, (o_copied, HEADS))
                        continue
                    if first_pair and s == 0:
                        norm_log_main(last)
                    if s == 1:
                        if first_pair:
                            norm_finish(last)
                        square_mix(vT[:, 0:T], i - 1, (conv_step, 4 * (i - HEADS)))
                    if s == 2:
                        norm_log_main(i - 1)
                    if s == 3:
                        norm_finish(i - 1)

            for u in range(2):
                head(0, u, u, u > 0, False)
            with act.Fori(1, HEADS // 2) as p:
                for u in range(2):
                    head(p, u, 2 * p + u, True, True)
            for u in range(2):
                group(HEADS // 2, u, HEADS + u, first_pair=True)
            with act.Fori(HEADS // 2 + 1, (HEADS + GROUPS) // 2) as p:
                for u in range(2):
                    group(p, u, 2 * p + u)

            end = HEADS + GROUPS

            def mix_high(c):
                act.wait_ge((first_used, chunk_done)[c // TK], 3 * end)
                act.wait_ge(mixed, c + 1)
                nc.scalar.copy(act_hi[:, c, LATE], wide_c[:, c, LATE]).then_inc(mix_hi, 1)

            for c in range(TK):
                mix_high(c)
            round_weights((4, 0, T_OUT), LEAD)
            for c in range(TK, 10):
                mix_high(c)
            square_mix(vT[:, 0:T], end - 1, (conv_step, 4 * GROUPS))
            for c in range(10, KC - 1):
                mix_high(c)
            norm_log_main(end - 1)
            norm_finish(end - 1, bank_c)
            round_weights((4, 0, T_OUT), LEAD + 1)
            mix_high(KC - 1)
            act.wait_ge(ulast_copied, 1)
            rows = relu[0:4 * GROUPS, 0:P]
            act.dma_start(new_conv_prompt[0, 0].rearrange("a (g p) -> (a g) p", p=P), rows[0:2 * GROUPS, :])\
               .then_inc(conv_stored, 16)
            act.dma_start(new_conv_sample[0, 0].rearrange("a (g p) -> (a g) p", p=P),
                          rows[2 * GROUPS:4 * GROUPS, :]).then_inc(conv_stored, 16)

            def out_round(q, k_from, last=False):
                for k in range(4):
                    if k >= k_from:
                        round_weights((4, q, T_OUT), k + LEAD)
                    if k % 2:
                        c = 2 * q + k // 2
                        if last and k == 3:
                            load_log_table(1)
                        act.wait_ge(chunk_done, c + CH_OUT + 1)
                        square_row(acc_late[k // 2], 1, c, k // 2)
            act.wait_ge(mixed, end)
            out_round(0, 2)
            with act.Fori(1, KC // 2 - 1) as q:
                out_round(q, 0)
            out_round(KC // 2 - 1, 0, last=True)
            round_weights((FF_T, 0, T_FF), LEAD)

            make_rstd(1)
            act.wait_ge(chunk_done, CH_FF)
            for c in range(KC):
                act.wait_ge(*h2_made(c))
                A(act_hi[:, c, LATE], resid[:, c, LATE], ACT.Copy,
                  scale=cols[:, c + C_PREFFN:c + C_PREFFN + 1]).then_inc(f_hi, 1)
                if c == KC - 1:
                    load_log_table(2)
                square_row(resid[:, c, LATE], 2, c, c % 2)
                if c in (11, 15):
                    round_weights((FF_T, 0, T_FF), LEAD + 1 + c // 15)
            make_rstd(2)

            def ffn_block(b, first, last):
                phase = (FF_T, b, T_FF)
                ch = b * FF_CH + CH_FF
                for k in range(FF_T):
                    if not (first and k < 3) and not (last and k + LEAD >= FF_T):
                        round_weights(phase, k + LEAD)
                    f = k // 4
                    if f < FB and k % 4 == 1:
                        if first and f == 0:
                            act.wait_ge(gate_scaled, 1)
                        else:
                            act.wait_ge(chunk_copied, ch + 2 * f + 1)
                        A(buf_e[:, LATE], buf_g[:, LATE], ACT.Exp, scale=-1.0).then_inc(e_neg, 1)
                    if f < FB and k % 4 == 3:
                        act.wait_ge(chunk_copied, ch + 2 * f + 2)
                        nc.scalar.copy(ff_hi[:, f, LATE], buf_g[:, LATE]).then_inc(ff_hi_ready, 1)
                    if last and f >= FB:
                        for c in (2 * (k - 4 * FB), 2 * (k - 4 * FB) + 1):
                            if c == KC - 1:
                                load_log_table(3)
                            act.wait_ge(chunk_copied, ch + 2 * FB + c + 1)
                            square_row(wide_c[:, c, LATE], 3, c, c % 2)

            ffn_block(0, True, False)
            with act.Fori(1, NFB - 1) as b:
                ffn_block(b, False, False)
            ffn_block(NFB - 1, False, True)

            make_rstd(3)
            for c in range(KC):
                s = c % 4
                act.wait_ge(y_turned, c + 1)
                if c >= 4:
                    act.wait_ge(y_stored[s], 32 * (c // 4))
                A(y_tok[:, s, 0:3, :], ps[:, 2 * s, 0:3 * P].rearrange("p (j f) -> p j f", f=P), ACT.Copy)
                A(y_tok[:, s, 3, :], ps[:, 2 * s + 1, 0:P], ACT.Copy)
                A(y_tok[0:TS, s, QB, :], ps[0:TS, 2 * s + 1, P:2 * P], ACT.Copy)\
                    .then_inc(y_copied, 1)

        @block.vector
        def _(dve):
            V = nc.vector

            def column(at_col):
                return cols[:, bass.ds(at_col, 1)] if not known(at_col) else cols[:, at_col:at_col + 1]

            def in_halves(x):
                return x.rearrange("p (h t) -> p h t", h=2)

            def copy_chunk(no, par, out, scale=None):
                dve.wait_ge(chunk_done, no + 1)
                if out is qT:
                    ins = V.scalar_tensor_tensor(out=in_halves(out[:, LATE]), in0=acc_late[par],
                                                 scalar=1.0 if scale is None else scale,
                                                 in1=in_halves(rstd[:, LATE]), op0=ALU.mult, op1=ALU.mult)
                else:
                    ins = V.tensor_tensor(in_halves(out[:, 0:T]), acc[par], in_halves(rstd[:, :]), ALU.mult)
                ins.then_inc(chunk_copied, 1)

            def mix(n, src, at_col):
                dve.wait_ge(norm_ready, n + 1)
                out = wide_c[:, bass.ds(n, 1), LATE].rearrange("p c t -> p (c t)")
                V.scalar_tensor_tensor(out=out, in0=src[:, LATE], scalar=column(at_col), in1=buf_e[:, LATE],
                                       op0=ALU.mult, op1=ALU.mult).then_inc(mixed, 1)

            def rest_of_squares(n):
                dve.wait_ge(sq_hi_ready, n + 1)
                V.tensor_tensor(sq_lo, buf_e[:, NMETA:TP], sq_hi.bitcast(F32), ALU.subtract)\
                    .then_inc(sq_split, 1)

            def ends(a, par):
                dve.wait_ge(ends_turned, a + 1)
                V.tensor_copy(vtok[0:TAIL, par, QB, :], bank_d[0:TAIL, 0:P])
                V.tensor_copy(ktok[0:TAIL, QB, :], bank_d[0:TAIL, P:2 * P])
                V.tensor_copy(vtok[0:TS, par, QB + 1, :], bank_d[0:TS, 2 * P:3 * P])
                V.tensor_copy(ktok[0:TS, QB + 1, :], bank_d[0:TS, 3 * P:4 * P]).then_inc(ends_copied, 1)

            def softplus(a):
                dve.wait_ge(log_ready, a + 1)
                V.tensor_tensor(relu, relu, soft, ALU.add).then_inc(sp_made, 1)

            def softplus_rest(a):
                dve.wait_ge(sp_hi_ready, a + 1)
                V.tensor_tensor(sp_lo, relu, sp_hi.bitcast(F32), ALU.subtract).then_inc(sp_split, 1)

            def outputs(a):
                dve.wait_ge(o_ready, a + 1)
                V.tensor_copy(buf_g[:, NMETA:TP], bank_d)
                V.tensor_copy(buf_g[:, TP:T], bank_c[:, 0:TS]).then_inc(o_copied, 1)

            def conv(g):
                dve.wait_ge(u_ends, g + 1)
                taps = [column(g + C_CONVW + GROUPS * j) for j in range(3)]
                for j in range(3):
                    if j:
                        dve.wait_ge(conv_step, 4 * g + j)
                    for to, n, at_u in ((0, TP, 0), (TP, TS, TP + 2)):
                        x = uext[:, at_u + j:at_u + j + n]
                        if j == 0:
                            last = V.tensor_scalar(vT[:, to:to + n], x, taps[0], None, ALU.mult)
                        else:
                            last = V.scalar_tensor_tensor(out=vT[:, to:to + n], in0=x, scalar=taps[j],
                                                          in1=vT[:, to:to + n], op0=ALU.mult, op1=ALU.add)
                    last.then_inc(conv_step, 1)
                dve.wait_ge(conv_step, 4 * g + 3)
                V.tensor_tensor(vT[:, LATE], vT[:, LATE], qT[:, LATE], ALU.mult).then_inc(conv_step, 1)

            def conv_input(no, par, g):
                dve.wait_ge(chunk_done, no + 1)
                dve.wait_ge(c_scaled, g + 1)
                V.tensor_tensor(uext[:, 2:2 + HALF], acc[par][:, 0, :], kT[:, 0:HALF], ALU.mult)
                V.tensor_tensor(uext[:, 2 + HALF:2 + TP], acc[par][:, 1, 0:TP - HALF], kT[:, HALF:TP],
                                ALU.mult)
                V.tensor_tensor(uext[:, 4 + TP:4 + T], acc[par][:, 1, TP - HALF:HALF], kT[:, TP:T],
                                ALU.mult).then_inc(chunk_copied, 1)
                state = cols[:, C_STATE:C_STATE + 2 * GROUPS].rearrange("p (a g) -> p a g", a=2)
                V.tensor_copy(uext[:, 2 + TP:4 + TP].unsqueeze(2), state[:, :, bass.ds(g, 1)])
                dve.wait_ge(chunk_copied, no + 1)
                V.tensor_copy(ulast[:, 0:2, bass.ds(g, 1)], uext[:, TP:2 + TP].unsqueeze(2))
                V.tensor_copy(ulast[:, 2:4, bass.ds(g, 1)], uext[:, 2 + T:4 + T].unsqueeze(2))\
                    .then_inc(u_ends, 1)

            V.memset(eps[:, :], EPS)
            V.memset(sq_sums[:, :, :], 0.0).then_inc(const_ready, 1)

            def copy_left(c):
                dve.wait_ge(x_turned, c + 1)
                if c >= RING:
                    dve.wait_ge(h_stored[c % RING], 16 * (c // RING))
                V.tensor_copy(h_ring[:, c % RING, 0:3 * P], ps[:, 2 + 2 * (c % 3), 0:3 * P])\
                    .then_inc(h_left, 1)

            copy_left(0)
            dve.wait_ge(cols_turned, 1)
            V.tensor_copy(cols[:, :], bank_d[:, 0:NCOL]).then_inc(cols_ready, 1)
            rest_of_weights((PAIR_T, 0, 0), 0)
            dve.wait_ge(cols_ready, 1)
            for c in range(KC):
                s = c % RING
                if c + 1 < KC:
                    copy_left(c + 1)
                dve.wait_ge(x_hi_ready, c + 1)
                V.scalar_tensor_tensor(out=act_lo[:, c, :], in0=h_ring[:, s, :], scalar=column(C_PREMIX + c),
                                       in1=act_hi[:, c, :].bitcast(F32), op0=ALU.mult,
                                       op1=ALU.subtract).then_inc(x_ready, 1)
            dve.wait_ge(lo_ready, LEAD)
            for j in range(RING):
                dve.wait_ge(h_stored[j], 16 * (KC // RING))

            def diagonals():
                dve.wait_ge(x_squared, 2 * (QB + 1))
                V.tensor_tensor(sq_sums[:, 0, :], sq_sums[:, 0, :], sq_sums[:, 1, :], ALU.add)\
                    .then_inc(x_summed, 1)
                dve.wait_ge(x_summed, 1)
                for j in range(QB + 1):
                    n = P if j < QB else TAIL + TS
                    ins = V.tensor_scalar(buf_e[0:n, j * P:j * P + n], ident[0:n, 0:n],
                                          sq_sums[0:n, 0, j:j + 1], None, ALU.mult)
                ins.then_inc(diag_ready, 1)

            def head(p, u, i, has_attention, has_norm):
                a, n = i - 1, i - 2
                no = 3 * i
                for s in range(6):
                    if s == 1:
                        if has_attention:
                            softplus(a)
                        else:
                            dve.wait_ge(rstd_ready, 1)
                            V.memset(bank_b[:, BNN - B1:BANK], 0.0).then_inc(bank_b_clear, 1)
                            V.memset(uext[:, 0:2], 0.0)
                        dve.wait_ge(kc_turned, i + 1)
                        V.tensor_copy(kcT, bank_d[:, 0:2 * P]).then_inc(kc_copied, 1)
                        copy_chunk(no, (3 * u) % 2, vT)
                    if s == 0 and not has_attention:
                        diagonals()
                    rest_of_weights((PAIR_T, p, 0), 6 * u + s + LEAD)
                    if s == 0 and has_attention:
                        ends(a, (u + 1) % 2)
                    if s == 1:
                        if has_attention:
                            softplus_rest(a)
                        if has_norm:
                            mix(n, buf_g[:, :], n + C_ATTN)
                    if s == 2:
                        dve.wait_ge(v_turned, i + 1)
                        if has_norm:
                            dve.wait_ge(v_stored[u], 48 * p)
                        V.tensor_copy(vtok[:, u, 0:QB, :], bank_d.rearrange("p (j d) -> p j d", d=P))\
                            .then_inc(v_copied, 1)
                    if s == 3:
                        copy_chunk(no + 1, (3 * u + 1) % 2, kT)
                    if s == 4 and has_attention:
                        outputs(a)
                    if s == 5:
                        if has_attention:
                            rest_of_squares(a)
                        copy_chunk(no + 2, (3 * u + 2) % 2, qT, SCALE)
                        dve.wait_ge(k_turned, i + 1)
                        if has_attention:
                            dve.wait_ge(k_stored, 48 * i)
                        V.tensor_copy(ktok[:, 0:QB, :], bank_d.rearrange("p (j d) -> p j d", d=P))\
                            .then_inc(k_copied, 1)

            def group(p, u, i, first_pair=False):
                last, g, no = HEADS - 1, i - HEADS, 3 * i
                begins = first_pair and u == 0
                for s in range(6):
                    if s == 1 and begins:
                        softplus(last)
                    if s == 2 and not begins:
                        rest_of_squares(i - 1)
                    rest_of_weights((PAIR_T, p, 0), 6 * u + s + LEAD)
                    if s == 0:
                        if begins:
                            ends(last, last % 2)
                        else:
                            conv(g - 1)
                    if s == 1:
                        if not begins:
                            dve.wait_ge(conv_step, 4 * g)
                        copy_chunk(no, (3 * u) % 2, qT)
                        if begins:
                            softplus_rest(last)
                            mix(last - 1, buf_g[:, :], C_ATTN + last - 1)
                        elif first_pair:
                            mix(last, buf_g[:, :], C_ATTN + last)
                    if s == 3:
                        copy_chunk(no + 1, (3 * u + 1) % 2, kT)
                        dve.wait_ge(chunk_copied, no + 2)
                        V.tensor_tensor(kT[:, 0:T], kT[:, 0:T], rstd[:, :], ALU.mult).then_inc(c_scaled, 1)
                    if s == 4:
                        if begins:
                            outputs(last)
                        else:
                            mix(i - 1, vT[:, 0:T], g - 1 + C_CONV)
                    if s == 5:
                        if begins:
                            rest_of_squares(last)
                        conv_input(no + 2, (3 * u + 2) % 2, g)

            for u in range(2):
                head(0, u, u, u > 0, False)
            with dve.Fori(1, HEADS // 2) as p:
                for u in range(2):
                    head(p, u, 2 * p + u, True, True)
            for u in range(2):
                group(HEADS // 2, u, HEADS + u, first_pair=True)
            with dve.Fori(HEADS // 2 + 1, (HEADS + GROUPS) // 2) as p:
                for u in range(2):
                    group(p, u, 2 * p + u)

            def mix_rest(c):
                dve.wait_ge(mix_hi, c + 1)
                V.tensor_tensor(act_lo[:, c, LATE], wide_c[:, c, LATE], act_hi[:, c, LATE].bitcast(F32),
                                ALU.subtract).then_inc(mix_split[1], 1)

            conv(GROUPS - 1)
            rest_of_weights((4, 0, T_OUT), LEAD)
            for c in range(TK, KC - 1):
                mix_rest(c)
                if c == 9:
                    rest_of_squares(HEADS + GROUPS - 1)
            rest_of_weights((4, 0, T_OUT), LEAD + 1)
            mix(HEADS + GROUPS - 1, vT[:, 0:T], C_CONV + GROUPS - 1)
            mix_rest(KC - 1)
            dve.wait_ge(ulast_turned, 1)
            V.tensor_copy(relu[0:4 * GROUPS, 0:P], bank_a[0:4 * GROUPS, 0:P]).then_inc(ulast_copied, 1)

            def out_round(q, k_from):
                for k in range(4):
                    if k >= k_from:
                        rest_of_weights((4, q, T_OUT), k + LEAD)
                    if k % 2:
                        c = 2 * q + k // 2
                        dve.wait_ge(sq_made, c + 1)
                        out = wide_c[:, bass.ds(c, 1), LATE].rearrange("p c t -> p (c t)")
                        V.tensor_scalar(in_halves(out), acc_late[k // 2], column(c + C_POSTMIX), None,
                                        ALU.mult).then_inc(chunk_copied, 1)
            out_round(0, 2)
            with dve.Fori(1, KC // 2) as q:
                out_round(q, 0)

            def add_to_stream(c, multiplied, done):
                dve.wait_ge(multiplied, c + 1)
                V.tensor_tensor(resid[:, c, LATE], resid[:, c, LATE], wide_c[:, c, LATE], ALU.add)\
                    .then_inc(done[0], 1)

            rest_of_weights((FF_T, 0, T_FF), LEAD)
            dve.wait_ge(rstd_ready, 2)
            dve.wait_ge(h_loaded, 16)
            for c in range(-2, KC):
                if c + 2 < KC:
                    V.tensor_tensor(wide_c[:, c + 2, LATE], wide_c[:, c + 2, LATE], rstd[:, LATE], ALU.mult)\
                        .then_inc(scaled, 1)
                ahead = 0 if c == -2 else c + 1 if c >= 0 else KC
                if ahead < KC and h2_adder(ahead) == 0:
                    add_to_stream(ahead, scaled, h2_ready)
                if c >= 0:
                    dve.wait_ge(f_hi, c + 1)
                    V.scalar_tensor_tensor(out=act_lo[:, c, LATE], in0=resid[:, c, LATE],
                                           scalar=column(c + C_PREFFN), in1=act_hi[:, c, LATE].bitcast(F32),
                                           op0=ALU.mult, op1=ALU.subtract).then_inc(f_split, 1)
                if c == 12:
                    rest_of_weights((FF_T, 0, T_FF), LEAD + 1)

            gate, sigmoid, one_over_rms = buf_g[:, LATE], buf_e[:, LATE], rstd[:, LATE]

            def ffn_block(b, first, last):
                phase = (FF_T, b, T_FF)
                ch = b * FF_CH + CH_FF
                for k in range(FF_T):
                    if not (first and k < 3) and not (last and k + LEAD >= FF_T):
                        rest_of_weights(phase, k + LEAD)
                    f = k // 4
                    if f < FB:
                        if k % 4 == 1:
                            dve.wait_ge(chunk_done, ch + 2 * f + 1)
                            if first and f == 0:
                                V.tensor_copy(in_halves(wide_c[:, 0, LATE]), acc_late[0])\
                                    .then_inc(chunk_copied, 1)
                                rest_of_weights(phase, 2 + LEAD)
                                dve.wait_ge(chunk_copied, ch + 1)
                                dve.wait_ge(rstd_ready, 3)
                                V.tensor_tensor(gate, wide_c[:, 0, LATE], one_over_rms, ALU.mult)\
                                    .then_inc(gate_scaled, 1)
                            else:
                                dve.wait_ge(ff_ready, b * FB + f)
                                V.tensor_tensor(in_halves(gate), acc_late[0], in_halves(one_over_rms),
                                                ALU.mult).then_inc(chunk_copied, 1)
                        step = b * 4 * FB + 4 * f
                        if k % 4 == 2:
                            dve.wait_ge(e_neg, b * FB + f + 1)
                            V.tensor_scalar(sigmoid, sigmoid, 1.0, None, ALU.add).then_inc(ff_step, 1)
                            dve.wait_ge(ff_step, step + 1)
                            V.reciprocal(sigmoid, sigmoid).then_inc(ff_step, 1)
                            dve.wait_ge(ff_step, step + 2)
                            V.tensor_tensor(gate, gate, sigmoid, ALU.mult).then_inc(ff_step, 1)
                            dve.wait_ge(ff_step, step + 3)
                            V.tensor_tensor(gate, gate, one_over_rms, ALU.mult).then_inc(ff_step, 1)
                        if k % 4 == 3:
                            dve.wait_ge(ff_step, step + 4)
                            dve.wait_ge(chunk_done, ch + 2 * f + 2)
                            V.tensor_tensor(in_halves(gate), acc_late[1], in_halves(gate), ALU.mult)\
                                .then_inc(chunk_copied, 1)
                            dve.wait_ge(ff_hi_ready, b * FB + f + 1)
                            V.tensor_tensor(ff_lo[:, f, LATE], gate, ff_hi[:, f, LATE].bitcast(F32),
                                            ALU.subtract).then_inc(ff_ready, 1)
                    else:
                        for o in range(2):
                            c = 2 * (k - 4 * FB) + o
                            dve.wait_ge(chunk_done, ch + 2 * FB + c + 1)
                            y = in_halves(wide_c[:, c, LATE])
                            if first:
                                ins = V.tensor_copy(y, acc_late[o])
                            else:
                                ins = V.tensor_tensor(y, acc_late[o], y, ALU.add)
                            ins.then_inc(chunk_copied, 1)

            ffn_block(0, True, False)
            with dve.Fori(1, NFB - 1) as b:
                ffn_block(b, False, False)
            ffn_block(NFB - 1, False, True)

            dve.wait_ge(rstd_ready, 4)
            for c in range(-1, KC):
                if c + 1 < KC:
                    V.scalar_tensor_tensor(out=wide_c[:, c + 1, LATE], in0=wide_c[:, c + 1, LATE],
                                           scalar=column(c + 1 + C_POSTFFN), in1=one_over_rms,
                                           op0=ALU.mult, op1=ALU.mult).then_inc(y_scaled, 1)
                if c >= 0 and y_adder(c) == 0:
                    add_to_stream(c, y_scaled, y_ready)

        def add_square(pool, r, c):
            total, square = buf_g[:, LATE], squares[c % 2]
            pool.wait_ge(sq_made, KC * (r - 1) + c + 1)
            if c == 0:
                ins = nc.gpsimd.tensor_copy(total, square)
            else:
                pool.wait_ge(sq_added, (KC - 1) * (r - 1) + c)
                ins = nc.gpsimd.tensor_tensor(total, total, square, ALU.add)
            ins.then_inc(sq_added, 1)

        @block.gpsimd
        def _(pool):
            G = nc.gpsimd
            G.memset(neg1, -1.0).then_inc(const_ready, 1)
            G.memset(ident[:, :], 0.0).then_inc(pool_step, 1)
            pool.wait_ge(pool_step, 1)
            G.affine_select(out=ident[:, :], in_=ident[:, :], compare_op=ALU.not_equal, fill=1.0, base=0,
                            pattern=[[-1, P]], channel_multiplier=1).then_inc(const_ready, 1)
            pool.wait_ge(const_ready, 3)
            G.affine_select(out=tri_r[:, :], in_=neg1, compare_op=ALU.is_ge, fill=0.0, base=0,
                            pattern=[[-1, P]], channel_multiplier=1).then_inc(const_ready, 1)

            for k in range(1, LEAD):
                pool.wait_ge(lo_ready, k)
                rest_of_weights((PAIR_T, 0, 0), k, nc.gpsimd)

            def mask(buf, made, ready, heads):
                pool.wait_ge(x_squared, 2 * (QB + 1))
                pool.wait_ge(made, heads)
                for at_z, n, first in ((0, P, NMETA), (B1, P, 0), (B3, P, 0), (B2, P, 0), (BTT, TAIL, 0),
                                       (BNN, TS, 0)):
                    x = buf[0:n, at_z:at_z + n]
                    last = G.affine_select(out=x, in_=x, compare_op=ALU.is_gt, fill=0.0, base=first,
                                           pattern=[[1, n]], channel_multiplier=-1)
                last.then_inc(ready, 1)

            with pool.Fori(1, HEADS + 1) as heads:
                mask(relu, sp_made, sp_ready, heads)
                mask(soft, w_made, w_ready, heads)

            for c in range(TK):
                pool.wait_ge(mix_hi, c + 1)
                G.tensor_tensor(act_lo[:, c, LATE], wide_c[:, c, LATE], act_hi[:, c, LATE].bitcast(F32),
                                ALU.subtract).then_inc(mix_split[0], 1)

            for c in range(KC - 1):
                add_square(pool, 1, c)

            def add_to_stream(c, multiplied, done):
                pool.wait_ge(multiplied, c + 1)
                G.tensor_tensor(resid[:, c, LATE], resid[:, c, LATE], wide_c[:, c, LATE], ALU.add)\
                    .then_inc(done[1], 1)

            pool.wait_ge(h_loaded, 16)
            pool.wait_ge(ms_ready, 2)
            for c in range(KC + 1):
                if c < KC and h2_adder(c) == 1:
                    add_to_stream(c, scaled, h2_ready)
                if c >= 2:
                    add_square(pool, 2, c - 2)

            for c in range(KC - 1):
                add_square(pool, 3, c)
            for c in range(KC):
                if y_adder(c) == 1:
                    add_to_stream(c, y_scaled, y_ready)


_INS = ["x_prompt", "x_sample", "cache_k", "cache_v", "state_conv", "meta", "w_in", "w_out", "conv_w",
        "g_pre_mix", "g_post_mix", "g_attn_out", "g_conv_out", "g_pre_ffn", "g_post_ffn",
        "w_gate", "w_up", "w_down"]


def kernel(**inputs):
    import numpy as _np
    import concourse.bacc as _bacc
    from concourse import mybir as _mybir
    from concourse.bass_utils import run_bass_kernel_spmd as _run

    arrays = {f"in_{n}_dram": _np.ascontiguousarray(inputs[n]) for n in _INS}
    nc = _bacc.Bacc("TRN2", target_bir_lowering=False, num_devices=1)
    args = [nc.dram_tensor(n, a.shape, _mybir.dt.from_np(a.dtype), kind="ExternalInput").ap()
            for n, a in arrays.items()]
    _, seq, d = inputs["x_prompt"].shape
    _, ts, _ = inputs["x_sample"].shape
    tp = inputs["meta"].shape[0] + seq
    depth, _, _, heads, hd = inputs["cache_k"].shape
    state = inputs["state_conv"].shape
    outs = [(1, seq, d), (1, ts, d), (depth, 1, tp, heads, hd), (depth, 1, tp, heads, hd), state,
            (depth, 1, ts, heads, hd), (depth, 1, ts, heads, hd), state]
    for i, shape in enumerate(outs):
        args.append(nc.dram_tensor(f"out_{i}_dram", shape, _mybir.dt.float32, kind="ExternalOutput").ap())
    args.append(nc.dram_tensor("h_scratch", (128, d // 128, tp + ts), _mybir.dt.float32, kind="Internal").ap())
    build_layer(nc, *args)
    r = _run(nc, [arrays], core_ids=[0])
    return tuple(r.results[0][f"out_{i}_dram"] for i in range(len(outs)))
```
